# Optimizing a Trainium2 kernel written in Bass

```python
import math
import jax, jax.numpy as jnp
from jax import lax
import numpy as np

D_MODEL = 1024
BATCH = 1
SEQ = 256
DEPTH = 2

N_MIXERS = 2
N_SB_LAYERS = (DEPTH + 1) // 2
N_MLA_LAYERS = DEPTH // 2
Q_BLOCK = 128
EPS = 1e-6

SB_HEADS = 16
SB_HEAD_DIM = D_MODEL // SB_HEADS

MLA_HEADS = 16
MLA_Q_LORA = 256
MLA_KV_LORA = 128
MLA_NOPE_DIM = 64
MLA_ROPE_DIM = 32
MLA_V_DIM = 64
ROPE_THETA = 10000.0

D_FF = 2816
FFN_RESIDUAL_WEIGHT = 0.5
N_NORMS_PER_LAYER = 6


def rms_norm(x, g):
    xf = x.astype(jnp.float32)
    y = xf * lax.rsqrt(jnp.mean(xf * xf, axis=-1, keepdims=True) + EPS)
    return (y * g.astype(jnp.float32)).astype(x.dtype)

def swiglu(x, w_in, w_out):
    gate, up = jnp.split(x @ w_in, 2, axis=-1)
    return (jax.nn.silu(gate) * up) @ w_out

def apply_rope(x, positions):
    d = x.shape[-1]
    inv_freq = ROPE_THETA ** (-jnp.arange(0, d, 2, dtype=jnp.float32) / d)
    ang = positions.astype(jnp.float32)[..., None] * inv_freq
    cos = jnp.cos(ang)[:, :, None, :].astype(x.dtype)
    sin = jnp.sin(ang)[:, :, None, :].astype(x.dtype)
    x1, x2 = jnp.split(x, 2, axis=-1)
    return jnp.concatenate([x1 * cos - x2 * sin, x2 * cos + x1 * sin], axis=-1)

def query_blocks(q):
    b, s, h, d = q.shape
    return q.reshape(b, s // Q_BLOCK, Q_BLOCK, h, d).transpose(1, 0, 2, 3, 4)

def merge_blocks(o):
    nb, b, qb, h, dv = o.shape
    return o.transpose(1, 0, 2, 3, 4).reshape(b, nb * qb, h * dv)

def stick_breaking_attention(h, w_in, w_out):
    b, s, _ = h.shape
    qkv = (h @ w_in).reshape(b, s, 3, SB_HEADS, SB_HEAD_DIM)
    q, k, v = qkv[:, :, 0], qkv[:, :, 1], qkv[:, :, 2]
    scale = 1.0 / math.sqrt(SB_HEAD_DIM)
    k_idx = jnp.arange(s)

    def block(args):
        qb, bi = args
        q_idx = bi * Q_BLOCK + jnp.arange(Q_BLOCK)
        z = jnp.einsum('bqhd,bkhd->bhqk', qb, k).astype(jnp.float32) * scale
        mask = k_idx[None, :] < q_idx[:, None]
        sp = jnp.where(mask, jax.nn.softplus(z), 0.0)
        tail = lax.cumsum(sp, axis=sp.ndim - 1, reverse=True) - sp
        log_a = jax.nn.log_sigmoid(z) - tail
        a = jnp.where(mask, jnp.exp(log_a), 0.0).astype(v.dtype)
        return jnp.einsum('bhqk,bkhd->bqhd', a, v)

    nb = s // Q_BLOCK
    o = lax.map(block, (query_blocks(q), jnp.arange(nb)))
    return merge_blocks(o) @ w_out

def multi_head_latent_attention(h, positions, w_in, q_norm, w_uq, kv_norm, w_ukv, w_out):
    b, s, _ = h.shape
    proj = h @ w_in
    c_q = proj[..., :MLA_Q_LORA]
    c_kv = proj[..., MLA_Q_LORA:MLA_Q_LORA + MLA_KV_LORA]
    k_rope = proj[..., MLA_Q_LORA + MLA_KV_LORA:][:, :, None, :]
    k_rope = apply_rope(k_rope, positions)[:, :, 0, :]

    q = (rms_norm(c_q, q_norm) @ w_uq).reshape(b, s, MLA_HEADS, MLA_NOPE_DIM + MLA_ROPE_DIM)
    q_nope = q[..., :MLA_NOPE_DIM]
    q_rope = apply_rope(q[..., MLA_NOPE_DIM:], positions)
    q = jnp.concatenate([q_nope, q_rope], axis=-1)

    kv = (rms_norm(c_kv, kv_norm) @ w_ukv).reshape(b, s, MLA_HEADS, MLA_NOPE_DIM + MLA_V_DIM)
    k_nope = kv[..., :MLA_NOPE_DIM]
    v = kv[..., MLA_NOPE_DIM:]
    scale = 1.0 / math.sqrt(MLA_NOPE_DIM + MLA_ROPE_DIM)
    k_idx = jnp.arange(s)

    def block(args):
        qb, bi = args
        q_idx = bi * Q_BLOCK + jnp.arange(Q_BLOCK)
        qn, qr = qb[..., :MLA_NOPE_DIM], qb[..., MLA_NOPE_DIM:]
        scores = (jnp.einsum('bqhd,bkhd->bhqk', qn, k_nope)
                  + jnp.einsum('bqhr,bkr->bhqk', qr, k_rope)).astype(jnp.float32) * scale
        mask = k_idx[None, :] <= q_idx[:, None]
        scores = jnp.where(mask, scores, -jnp.inf)
        p = jax.nn.softmax(scores, axis=-1).astype(v.dtype)
        return jnp.einsum('bhqk,bkhd->bqhd', p, v)

    nb = s // Q_BLOCK
    o = lax.map(block, (query_blocks(q), jnp.arange(nb)))
    return merge_blocks(o) @ w_out

def first_inputs(seed: int = 0) -> dict:
    key = jax.random.key(seed)
    ks = jax.random.split(key, 16)

    def w(k, shape, fan_in):
        return jax.random.normal(k, shape, jnp.float32) * fan_in ** -0.5

    def gain(k, shape):
        return 1.0 + 0.05 * jax.random.normal(k, shape, jnp.float32)

    sb_width = SB_HEADS * SB_HEAD_DIM
    mla_in = MLA_Q_LORA + MLA_KV_LORA + MLA_ROPE_DIM
    return {
        "x": jax.random.normal(ks[0], (BATCH, SEQ, D_MODEL), jnp.float32),
        "positions": jnp.broadcast_to(jnp.arange(SEQ, dtype=jnp.int32)[None, :], (BATCH, SEQ)),
        "norm_g": gain(ks[1], (DEPTH, N_NORMS_PER_LAYER, D_MODEL)),
        "ffn_w_in": w(ks[2], (DEPTH, 2, D_MODEL, 2 * D_FF), D_MODEL),
        "ffn_w_out": w(ks[3], (DEPTH, 2, D_FF, D_MODEL), D_FF),
        "sb_w_in": w(ks[4], (N_SB_LAYERS, D_MODEL, 3 * sb_width), D_MODEL),
        "sb_w_out": w(ks[5], (N_SB_LAYERS, sb_width, D_MODEL), sb_width),
        "mla_w_in": w(ks[6], (N_MLA_LAYERS, D_MODEL, mla_in), D_MODEL),
        "mla_q_norm": gain(ks[7], (N_MLA_LAYERS, MLA_Q_LORA)),
        "mla_w_uq": w(ks[8], (N_MLA_LAYERS, MLA_Q_LORA, MLA_HEADS * (MLA_NOPE_DIM + MLA_ROPE_DIM)), MLA_Q_LORA),
        "mla_kv_norm": gain(ks[9], (N_MLA_LAYERS, MLA_KV_LORA)),
        "mla_w_ukv": w(ks[10], (N_MLA_LAYERS, MLA_KV_LORA, MLA_HEADS * (MLA_NOPE_DIM + MLA_V_DIM)), MLA_KV_LORA),
        "mla_w_out": w(ks[11], (N_MLA_LAYERS, MLA_HEADS * MLA_V_DIM, D_MODEL), MLA_HEADS * MLA_V_DIM),
    }

def first_block(x, positions, norm_g, ffn_w_in, ffn_w_out, sb_w_in, sb_w_out,
              mla_w_in, mla_q_norm, mla_w_uq, mla_kv_norm, mla_w_ukv, mla_w_out):
    for i in range(DEPTH):
        g = norm_g[i]
        f = swiglu(rms_norm(x, g[0]), ffn_w_in[i, 0], ffn_w_out[i, 0])
        x = x + FFN_RESIDUAL_WEIGHT * rms_norm(f, g[1])
        h = rms_norm(x, g[2])
        j = i // N_MIXERS
        if i % N_MIXERS == 0:
            m = stick_breaking_attention(h, sb_w_in[j], sb_w_out[j])
        else:
            m = multi_head_latent_attention(h, positions, mla_w_in[j], mla_q_norm[j], mla_w_uq[j],
                                            mla_kv_norm[j], mla_w_ukv[j], mla_w_out[j])
        x = x + rms_norm(m, g[3])
        f = swiglu(rms_norm(x, g[4]), ffn_w_in[i, 1], ffn_w_out[i, 1])
        x = x + FFN_RESIDUAL_WEIGHT * rms_norm(f, g[5])
    return x


N_A_LAYERS = DEPTH // 2
N_B_LAYERS = DEPTH - N_A_LAYERS
M_HEADS = 4
M_DV = D_MODEL // M_HEADS
M_DK = M_DV // 2
M_CHUNK = 64
GATE_CAP = 15.0
M_QK_W = M_HEADS * M_DK
M_V_W = M_HEADS * M_DV
M_IN_COLS = 2 * M_QK_W + 2 * M_V_W + 2 * M_HEADS
M_SPLITS = [M_QK_W, 2 * M_QK_W, 2 * M_QK_W + M_V_W, 2 * M_QK_W + 2 * M_V_W, 2 * M_QK_W + 2 * M_V_W + M_HEADS]
A_HEAD_DIM = 64
A_Q_HEADS = D_MODEL // A_HEAD_DIM
A_KV_HEADS = 4
A_GROUP = A_Q_HEADS // A_KV_HEADS
WINDOW = 128
ROPE_DIM = A_HEAD_DIM // 4
ROPE_THETA_2 = 500000.0
D_FF_2 = 4 * D_MODEL
PLE_DIM = 256
LN_EPS = 1e-5
DEEPNORM_ALPHA = (2 * DEPTH) ** 0.25
DEEPNORM_BETA = (8 * DEPTH) ** -0.25


def layer_norm(x, g, b):
    xf = x.astype(jnp.float32)
    mu = jnp.mean(xf, axis=-1, keepdims=True)
    var = jnp.mean(jnp.square(xf - mu), axis=-1, keepdims=True)
    return ((xf - mu) * lax.rsqrt(var + LN_EPS) * g + b).astype(x.dtype)

def partial_rope(t, pos):
    half = ROPE_DIM // 2
    inv_freq = jnp.power(ROPE_THETA_2, -jnp.arange(half, dtype=jnp.float32) * (2.0 / ROPE_DIM))
    ang = pos.astype(jnp.float32)[..., None] * inv_freq
    cos = jnp.cos(ang)[:, :, None, :]
    sin = jnp.sin(ang)[:, :, None, :]
    tr = t[..., :ROPE_DIM].astype(jnp.float32)
    t1, t2 = tr[..., :half], tr[..., half:]
    rot = jnp.concatenate([t1 * cos - t2 * sin, t2 * cos + t1 * sin], axis=-1).astype(t.dtype)
    return jnp.concatenate([rot, t[..., ROPE_DIM:]], axis=-1)

def soft_cap(g):
    return GATE_CAP * jnp.tanh(g / GATE_CAP)

def to_chunks(t, nc):
    t = t.reshape(t.shape[0], nc, M_CHUNK, *t.shape[2:])
    return jnp.moveaxis(t, (1, 3), (0, 2))

def mlstm_chunkwise(q, k, v, ig, lf):
    B, S, H, DK = q.shape
    DV = v.shape[-1]
    nc = S // M_CHUNK
    xs = tuple(to_chunks(t, nc) for t in (q, k, v, ig, lf))
    causal = jnp.tril(jnp.ones((M_CHUNK, M_CHUNK), dtype=bool))
    init = (jnp.zeros((B, H, DK, DV), jnp.float32),
            jnp.zeros((B, H, DK), jnp.float32),
            jnp.zeros((B, H), jnp.float32))

    def step(carry, chunk):
        C, n, m = carry
        qc, kc, vc, igc, lfc = chunk
        b = jnp.cumsum(lfc, axis=-1)
        log_d = b[..., :, None] - b[..., None, :] + igc[..., None, :]
        log_d = jnp.where(causal, log_d, -jnp.inf)
        log_inter = b + m[..., None]
        m_t = jnp.maximum(jnp.max(log_d, axis=-1), log_inter)
        d = jnp.exp(log_d - m_t[..., None])
        inter = jnp.exp(log_inter - m_t)
        s = jnp.einsum('bhtk,bhsk->bhts', qc, kc) * d
        num = jnp.einsum('bhts,bhsv->bhtv', s, vc) + inter[..., None] * jnp.einsum('bhtk,bhkv->bhtv', qc, C)
        den = jnp.sum(s, axis=-1) + inter * jnp.einsum('bhtk,bhk->bht', qc, n)
        h = num / jnp.maximum(jnp.abs(den), jnp.exp(-m_t))[..., None]
        b_last = b[..., -1]
        a = b_last[..., None] - b + igc
        m_new = jnp.maximum(b_last + m, jnp.max(a, axis=-1))
        w = jnp.exp(a - m_new[..., None])
        decay = jnp.exp(b_last + m - m_new)
        C_new = decay[..., None, None] * C + jnp.einsum('bhs,bhsk,bhsv->bhkv', w, kc, vc)
        n_new = decay[..., None] * n + jnp.einsum('bhs,bhsk->bhk', w, kc)
        return (C_new, n_new, m_new), h

    _, h = lax.scan(step, init, xs)
    return jnp.moveaxis(h, (0, 2), (1, 3)).reshape(B, S, H, DV)

def mlstm_mixer(x, w_in, b_ig, b_fg, head_g, w_out):
    B, S, _ = x.shape
    proj = x @ w_in
    q, k, v, o, ig, fg = jnp.split(proj, M_SPLITS, axis=-1)
    q = q.reshape(B, S, M_HEADS, M_DK).astype(jnp.float32) * (M_DK ** -0.5)
    k = k.reshape(B, S, M_HEADS, M_DK).astype(jnp.float32)
    v = v.reshape(B, S, M_HEADS, M_DV).astype(jnp.float32)
    log_i = soft_cap(ig.astype(jnp.float32) + b_ig)
    log_f = jax.nn.log_sigmoid(soft_cap(fg.astype(jnp.float32) + b_fg))
    h = mlstm_chunkwise(q, k, v, log_i, log_f)
    mu = jnp.mean(h, axis=-1, keepdims=True)
    var = jnp.mean(jnp.square(h - mu), axis=-1, keepdims=True)
    h = (h - mu) * lax.rsqrt(var + LN_EPS) * head_g.reshape(M_HEADS, M_DV)
    h = h.reshape(B, S, D_MODEL).astype(x.dtype)
    return (jax.nn.sigmoid(o) * h) @ w_out

def shared_kv(x, pos, kv_w, kv_b):
    B, S, _ = x.shape
    kv = x @ kv_w + kv_b
    k, v = jnp.split(kv, 2, axis=-1)
    k = partial_rope(k.reshape(B, S, A_KV_HEADS, A_HEAD_DIM), pos)
    v = v.reshape(B, S, A_KV_HEADS, A_HEAD_DIM)
    return k, v

def banded(t, nb):
    t = t.reshape(t.shape[0], nb, WINDOW, A_KV_HEADS, A_HEAD_DIM)
    prev = jnp.pad(t, ((0, 0), (1, 0), (0, 0), (0, 0), (0, 0)))[:, :-1]
    return jnp.concatenate([prev, t], axis=2)

def swa_sink_attention(x, pos, k_sh, v_sh, w_q, b_q, sinks, w_o, b_o):
    B, S, _ = x.shape
    nb = S // WINDOW
    q = partial_rope((x @ w_q + b_q).reshape(B, S, A_Q_HEADS, A_HEAD_DIM), pos)
    q = q.reshape(B, nb, WINDOW, A_KV_HEADS, A_GROUP, A_HEAD_DIM)
    kb, vb = banded(k_sh, nb), banded(v_sh, nb)
    scores = jnp.einsum('bnqkgd,bnskd->bnkgqs', q, kb).astype(jnp.float32) * (A_HEAD_DIM ** -0.5)
    qi = jnp.arange(WINDOW)[:, None]
    si = jnp.arange(2 * WINDOW)[None, :]
    diff = qi + WINDOW - si
    band = (diff >= 0) & (diff < WINDOW)
    blk = jnp.arange(nb)[:, None, None]
    valid = band[None] & (blk * WINDOW - WINDOW + si[None] >= 0)
    scores = jnp.where(valid[None, :, None, None], scores, -jnp.inf)
    sink = sinks.astype(jnp.float32).reshape(A_KV_HEADS, A_GROUP)[None, None, :, :, None]
    m = jnp.maximum(jnp.max(scores, axis=-1), sink)
    e = jnp.exp(scores - m[..., None])
    probs = e / (jnp.sum(e, axis=-1) + jnp.exp(sink - m))[..., None]
    out = jnp.einsum('bnkgqs,bnskd->bnqkgd', probs.astype(x.dtype), vb).reshape(B, S, D_MODEL)
    return out @ w_o + b_o

def squared_relu_mlp(x, w_up, w_down):
    return jnp.square(jax.nn.relu(x @ w_up)) @ w_down

def second_inputs(seed: int = 0) -> dict:
    key = jax.random.key(seed)
    ks = jax.random.split(key, 24)
    f32 = jnp.float32
    nrm = lambda k, shape, scale: jax.random.normal(k, shape, f32) * scale
    x = jax.random.normal(ks[0], (BATCH, SEQ, D_MODEL), f32)
    p = jax.random.normal(ks[1], (DEPTH, BATCH, SEQ, PLE_DIM), f32)
    start = jax.random.randint(ks[2], (BATCH, 1), 0, 1024, dtype=jnp.int32)
    positions = (start + jnp.arange(SEQ, dtype=jnp.int32)[None, :]).astype(jnp.int32)
    a_w_in = nrm(ks[3], (N_A_LAYERS, D_MODEL, M_IN_COLS), D_MODEL ** -0.5)
    a_b_igate = nrm(ks[4], (N_A_LAYERS, M_HEADS), 0.1)
    a_b_fgate = jnp.linspace(3.0, 6.0, M_HEADS, dtype=f32)[None, :] + nrm(ks[5], (N_A_LAYERS, M_HEADS), 0.1)
    a_head_norm_g = 1.0 + nrm(ks[6], (N_A_LAYERS, D_MODEL), 0.02)
    a_w_out = nrm(ks[7], (N_A_LAYERS, D_MODEL, D_MODEL), D_MODEL ** -0.5 * DEEPNORM_BETA)
    kv_w = nrm(ks[8], (D_MODEL, 2 * A_KV_HEADS * A_HEAD_DIM), D_MODEL ** -0.5)
    kv_b = nrm(ks[9], (2 * A_KV_HEADS * A_HEAD_DIM,), 0.02)
    b_w_q = nrm(ks[10], (N_B_LAYERS, D_MODEL, A_Q_HEADS * A_HEAD_DIM), D_MODEL ** -0.5)
    b_b_q = nrm(ks[11], (N_B_LAYERS, A_Q_HEADS * A_HEAD_DIM), 0.02)
    b_sinks = nrm(ks[12], (N_B_LAYERS, A_Q_HEADS), 0.5)
    b_w_o = nrm(ks[13], (N_B_LAYERS, A_Q_HEADS * A_HEAD_DIM, D_MODEL), D_MODEL ** -0.5 * DEEPNORM_BETA)
    b_b_o = nrm(ks[14], (N_B_LAYERS, D_MODEL), 0.02)
    mix_ln_g = 1.0 + nrm(ks[15], (DEPTH, D_MODEL), 0.02)
    mix_ln_b = nrm(ks[16], (DEPTH, D_MODEL), 0.02)
    mlp_w_up = nrm(ks[17], (DEPTH, D_MODEL, D_FF_2), D_MODEL ** -0.5)
    mlp_w_down = nrm(ks[18], (DEPTH, D_FF_2, D_MODEL), D_FF_2 ** -0.5 * DEEPNORM_BETA)
    mlp_ln_g = 1.0 + nrm(ks[19], (DEPTH, D_MODEL), 0.02)
    mlp_ln_b = nrm(ks[20], (DEPTH, D_MODEL), 0.02)
    ple_w_gate = nrm(ks[21], (DEPTH, D_MODEL, D_MODEL), D_MODEL ** -0.5)
    ple_b_gate = nrm(ks[22], (DEPTH, D_MODEL), 0.02)
    ple_w_proj = nrm(ks[23], (DEPTH, PLE_DIM, D_MODEL), PLE_DIM ** -0.5 * DEEPNORM_BETA)
    return {"x": x, "p": p, "positions": positions,
            "a_w_in": a_w_in, "a_b_igate": a_b_igate, "a_b_fgate": a_b_fgate,
            "a_head_norm_g": a_head_norm_g, "a_w_out": a_w_out,
            "kv_w": kv_w, "kv_b": kv_b,
            "b_w_q": b_w_q, "b_b_q": b_b_q, "b_sinks": b_sinks, "b_w_o": b_w_o, "b_b_o": b_b_o,
            "mix_ln_g": mix_ln_g, "mix_ln_b": mix_ln_b,
            "mlp_w_up": mlp_w_up, "mlp_w_down": mlp_w_down, "mlp_ln_g": mlp_ln_g, "mlp_ln_b": mlp_ln_b,
            "ple_w_gate": ple_w_gate, "ple_b_gate": ple_b_gate, "ple_w_proj": ple_w_proj}

def second_block(x, p, positions, a_w_in, a_b_igate, a_b_fgate, a_head_norm_g, a_w_out,
              kv_w, kv_b, b_w_q, b_b_q, b_sinks, b_w_o, b_b_o,
              mix_ln_g, mix_ln_b, mlp_w_up, mlp_w_down, mlp_ln_g, mlp_ln_b,
              ple_w_gate, ple_b_gate, ple_w_proj):
    k_sh, v_sh = None, None
    for i in range(DEPTH):
        if i < N_A_LAYERS:
            mix = mlstm_mixer(x, a_w_in[i], a_b_igate[i], a_b_fgate[i], a_head_norm_g[i], a_w_out[i])
        else:
            if i == N_A_LAYERS:
                k_sh, v_sh = shared_kv(x, positions, kv_w, kv_b)
            j = i - N_A_LAYERS
            mix = swa_sink_attention(x, positions, k_sh, v_sh, b_w_q[j], b_b_q[j], b_sinks[j], b_w_o[j], b_b_o[j])
        x = layer_norm(DEEPNORM_ALPHA * x + mix, mix_ln_g[i], mix_ln_b[i])
        x = layer_norm(DEEPNORM_ALPHA * x + squared_relu_mlp(x, mlp_w_up[i], mlp_w_down[i]), mlp_ln_g[i], mlp_ln_b[i])
        x = x + jax.nn.sigmoid(x @ ple_w_gate[i] + ple_b_gate[i]) * (p[i] @ ple_w_proj[i])
    return x


def setup_inputs(seed=0):
    out = dict(first_inputs(seed))
    for name, value in second_inputs(seed + 1).items():
        if name != "x":
            out[name + "_2"] = value
    return out


def reference(
    x, positions, norm_g, ffn_w_in, ffn_w_out, sb_w_in, sb_w_out, mla_w_in, mla_q_norm,
    mla_w_uq, mla_kv_norm, mla_w_ukv, mla_w_out, p_2, positions_2, a_w_in_2, a_b_igate_2,
    a_b_fgate_2, a_head_norm_g_2, a_w_out_2, kv_w_2, kv_b_2, b_w_q_2, b_b_q_2, b_sinks_2,
    b_w_o_2, b_b_o_2, mix_ln_g_2, mix_ln_b_2, mlp_w_up_2, mlp_w_down_2, mlp_ln_g_2, mlp_ln_b_2,
    ple_w_gate_2, ple_b_gate_2, ple_w_proj_2,
):
    x = first_block(
        x, positions, norm_g, ffn_w_in, ffn_w_out, sb_w_in, sb_w_out, mla_w_in, mla_q_norm,
        mla_w_uq, mla_kv_norm, mla_w_ukv, mla_w_out,
    )
    return second_block(
        x, p_2, positions_2, a_w_in_2, a_b_igate_2, a_b_fgate_2, a_head_norm_g_2, a_w_out_2,
        kv_w_2, kv_b_2, b_w_q_2, b_b_q_2, b_sinks_2, b_w_o_2, b_b_o_2, mix_ln_g_2, mix_ln_b_2,
        mlp_w_up_2, mlp_w_down_2, mlp_ln_g_2, mlp_ln_b_2, ple_w_gate_2, ple_b_gate_2,
        ple_w_proj_2,
    )


_drawn_inputs = setup_inputs


def setup_inputs(seed=0):
    import zlib

    import numpy as np

    out = dict(_drawn_inputs(seed))
    spreads = {}
    factors = {'a_b_igate_2': 64.0,
     'a_head_norm_g_2': 36.907,
     'kv_b_2': 8.0,
     'b_b_q_2': 50.167,
     'b_sinks_2': 8.0,
     'b_b_o_2': 4.262,
     'ple_b_gate_2': 8.0}
    for name, (base, spread) in spreads.items():
        noise = np.random.default_rng([zlib.crc32(name.encode()), seed]).standard_normal(out[name].shape)
        drawn = base * np.exp(spread * noise) if base else spread * noise
        out[name] = __import__('jax').numpy.asarray(drawn.astype(out[name].dtype))
    for name, factor in factors.items():
        out[name] = (out[name] * factor).astype(out[name].dtype)
    return out
```

```python
from contextlib import ExitStack

import numpy as np

import concourse.bass as bass
from concourse import mybir

F32 = mybir.dt.float32
F32R = mybir.dt.float32r
I32 = mybir.dt.int32
ALU = mybir.AluOpType
ACT = mybir.ActivationFunctionType
AX = mybir.AxisListType

P = 128
S = 256
T = S // P
D = 1024
KD = D // P
BANK = 512
RING = 3
UNIT = 2048
GW = 256
FF = 2816
FG = FF // GW
FF2 = 4096
MG = FF2 // GW
EPS = 1e-6
LN_EPS = 1e-5
LOOP_UNITS = 6
FFN_FIRST, FFN_BODY, FFN_TRIPS = 3, 2, 4
MLP_FIRST, MLP_BODY, MLP_TRIPS = 4, 3, 4
HEADS = 16
HD = 64
PAIRS = HEADS // 2
QB = 3 * P
NG = 12 * KD + 3
Q_LORA, KV_LORA, ROPE, NOPE = 256, 128, 32, 64
MLA_IN = Q_LORA + KV_LORA + ROPE
MLA_W = NOPE + ROPE
KV_HEADS = 4
ROPE2 = 16
M_HEADS = 4
M_DK = 128
M_DV = 256
GATE_CAP = 15.0
PLE = 256
ALPHA = 4 ** 0.25
MASKED = -1e30
INV_TURN = float(1 / (2 * np.pi))
TURN_PARTS = (6.28125, 2029 / 2 ** 20, float(2 * np.pi - 6.28125 - 2029 / 2 ** 20))
SIN_MAX = 3.1415925

STAGE_UNITS = {"ffn": 3 * FG, "sb": 16, "mla": 9, "mlstm": 17, "swa": 10, "mlp": 2 * MG, "ple": 5}
VECTORS_USED = {"ffn": 1, "sb": 1, "mla": 1, "mlstm": 3, "swa": 5, "mlp": 2, "ple": 1}
STAGES = ["ffn", "sb", "ffn", "ffn", "mla", "ffn", "mlstm", "mlp", "ple", "swa", "mlp", "ple"]


class Chain:

    def __init__(self, eng, sem):
        self.eng, self.sem, self.n = eng, sem, 0

    def link(self, ins):
        self.n += 1
        ins.then_inc(self.sem, 1)
        self.eng.wait_ge(self.sem, self.n)

    def count(self, ins):
        self.n += 1
        ins.then_inc(self.sem, 1)


def inverse_frequencies(theta, width):
    return (np.float32(theta) ** (-(np.arange(0, width, 2, dtype=np.float32) / np.float32(width)))).astype(np.float32)


def build(nc, a, out):
    ctx = ExitStack()
    with ctx:
        def sb(name, shape, dt=F32):
            return ctx.enter_context(nc.sbuf_tensor(name, shape, dt))

        def sem(name):
            return ctx.enter_context(nc.semaphore(name))

        x = sb("x_rows", [P, T, D])
        xn = sb("scratch_rows", [P, T, D])
        xTh = sb("turned_high", [P, KD, S], F32R)
        xTl = sb("turned_low", [P, KD, S], F32R)
        raw = sb("weights_raw", [P, RING, UNIT])
        whi = sb("weights_high", [P, RING, UNIT], F32R)
        wlo = sb("weights_low", [P, RING, UNIT], F32R)
        hTh = sb("hidden_high", [P, 3, 2, S], F32R)
        hTl = sb("hidden_low", [P, 3, 2, S], F32R)
        hid = sb("hidden", [P, 3, BANK])
        vec = sb("row_vectors", [P, 3, D])
        gain_rows = sb("gain_rows", [NG, P])
        gain_cols = sb("gain_columns", [P, NG])
        square_out = sb("square_out", [P, T, D])
        ident = sb("identity", [P, P])
        stat = sb("stat", [P, 64])
        work = sb("work", [P, 13312])
        probs_T = sb("probs_turned", [P, 2, QB])
        neg_tri = sb("minus_lower", [P, P])
        neg_ones = sb("minus_ones", [P, P])
        later = sb("later_mask", [P, P])
        causal = sb("causal_bias", [P, QB])
        window = sb("window_bias", [P, QB])
        pos_i = sb("positions_int", [4, P], I32)
        pos_rows = sb("positions_rows", [4, P])
        pos = sb("positions", [P, 4])
        inv_freq = sb("inverse_frequencies", [P, 24])
        angle = sb("angle", [P, 96])
        turns = sb("whole_turns", [P, 96])
        turns_i = sb("whole_turns_int", [P, 96], I32)
        trig = sb("sines_cosines", [P, 96])
        att_stat = sb("attention_stat", [P, 5, 2 * HEADS])
        sinks = sb("sinks", [P, HEADS])
        minus_sinks = sb("minus_sinks", [P, HEADS])
        gate_bias = sb("gate_bias", [P, 2 * M_HEADS])
        ml_small = sb("mlstm_small", [P, 152])

        acc = ctx.enter_context(nc.psum_tensor("acc", [P, T, D], F32))
        wk = ctx.enter_context(nc.psum_tensor("wk", [P, 4, BANK], F32))

        landed = [sem(f"unit_landed_{s}") for s in range(RING)]
        high_ready = sem("unit_high_ready")
        unit_ready = sem("unit_ready")
        unit_done = sem("unit_done")
        x_loaded = sem("x_loaded")
        x_ready = sem("x_ready")
        gains_loaded = sem("gains_loaded")
        gains_turned = sem("gains_turned")
        gains_kept = sem("gains_kept")
        vec_loaded = [sem(f"vec_loaded_{s}") for s in range(3)]
        ident_ready = sem("ident_ready")
        squares_ready = sem("squares_ready")
        scale_ready = sem("rms_scale_ready")
        rows_v = sem("rows_ready_dve")
        rows_a = sem("rows_ready_act")
        turned = sem("turned")
        turned_high = sem("turned_high_ready")
        turned_kept = sem("turned_kept")
        act_ready = sem("activation_ready")
        hidden_made = sem("hidden_made")
        hidden_high = sem("hidden_high_ready")
        hidden_ready = sem("hidden_ready")
        act_chain = sem("act_chain")
        dve_chain = sem("dve_chain")
        pool_chain = sem("pool_chain")
        pool_order = sem("pool_order")
        out_stored = sem("out_stored")
        pos_loaded = sem("positions_loaded")
        pos_made = sem("positions_float")
        pos_turned = sem("positions_turned")
        angles_ready = sem("angles_ready")
        trig_ready = sem("trig_ready")
        masks_ready = sem("masks_ready")
        freq_ready = sem("frequencies_ready")
        bias_ready = sem("bias_masks_ready")
        sinks_loaded = sem("sinks_loaded")
        mixed = sem("mixed")
        sbs = {n: sem("sb_" + n) for n in (
            "v_kept", "q_kept", "k_kept", "z_ready", "abs_ready", "log_ready", "softplus_ready", "logits_ready",
            "raw_ready", "weights_ready", "out_ready", "out_high", "out_kept")}

        block = ctx.enter_context(nc.Block())

        x_d = a["x"].rearrange("b (t p) d -> p (b t) d", p=P)
        out_d = out.rearrange("b (t p) d -> p (b t) d", p=P)

        def col_units(w):
            return w.rearrange("(k p) (g n) -> g p k n", p=P, n=GW)

        def row_units(w):
            return w.rearrange("(g k p) n -> g p k n", p=P, k=2)

        def quarter_units(w):
            return w.rearrange("(h k p) (c n) -> h c p k n", p=P, k=4, n=BANK)

        ffn_in = [[col_units(a["ffn_w_in"][l, f]) for f in range(2)] for l in range(2)]
        ffn_out = [[row_units(a["ffn_w_out"][l, f]) for f in range(2)] for l in range(2)]
        mlp_up = [col_units(a["mlp_w_up_2"][l]) for l in range(2)]
        mlp_down = [row_units(a["mlp_w_down_2"][l]) for l in range(2)]
        g = a["norm_g"]

        def row_vectors(name, n):
            return {"ffn": lambda: [g[n // 2, 1 + 4 * (n % 2)]], "sb": lambda: [g[0, 3]], "mla": lambda: [g[1, 3]],
                    "mlstm": lambda: [a["a_head_norm_g_2"][0], a["mix_ln_g_2"][0], a["mix_ln_b_2"][0]],
                    "swa": lambda: [a["kv_b_2"], a["b_b_q_2"][0], a["b_b_o_2"][0], a["mix_ln_g_2"][1], a["mix_ln_b_2"][1]],
                    "mlp": lambda: [a["mlp_ln_g_2"][n], a["mlp_ln_b_2"][n]], "ple": lambda: [a["ple_b_gate_2"][n]]}[name]()

        VECTORS = [(v, s, j) for s, name in enumerate(STAGES)
                   for j, v in enumerate(row_vectors(name, STAGES[:s].count(name)))]

        plan, at = [], 0
        for n, name in enumerate(STAGES):
            plan.append((name, at, STAGES[:n].count(name)))
            at += STAGE_UNITS[name]
        TOTAL = at

        def slot(tensor, u, k):
            return tensor[:, u % RING, :].rearrange("p (k n) -> p k n", k=k)

        def ffn_units(U, r):
            return U + max(3 * r - 1, 0), U + max(3 * r, 1), U + 3 * r + 1

        def mlp_units(U, r):
            return U + max(2 * r - 1, 0), U + 2 * r

        sb_q = work[:, 0:2048].rearrange("p (j s) -> p j s", s=S)
        sb_k = work[:, 2048:4096].rearrange("p (j s) -> p j s", s=S)
        sb_v = work[:, 4096:6144].rearrange("p (t d) -> p t d", t=T)
        sb_a = work[:, 6144:6144 + 2 * QB].rearrange("p (b n) -> p b n", b=2)

        mla_q = work[:, 0:3072].rearrange("p (t h w) -> p t h w", t=T, h=HEADS)
        mla_qT = work[0:MLA_W, 3072:7168].rearrange("p (h s) -> p h s", s=S)
        mla_kT = work[0:MLA_W, 7168:11264].rearrange("p (h s) -> p h s", s=S)
        mla_v = work[:, 11264:13312].rearrange("p (t d) -> p t d", t=T)
        swa_q = work[:, 0:2048].rearrange("p (t h w) -> p t h w", t=T, h=HEADS)
        swa_kv = work[:, 2048:3072].rearrange("p (t n) -> p t n", t=T)
        swa_qT = work[0:HD, 3072:7168].rearrange("p (h s) -> p h s", s=S)
        swa_kT = work[0:HD, 7168:8192].rearrange("p (h s) -> p h s", s=S)
        ml_q = work[:, 0:1024].rearrange("p (h s) -> p h s", s=S)
        ml_k = work[:, 1024:2048].rearrange("p (h s) -> p h s", s=S)
        ml_v = work[:, 2048:4096].rearrange("p (t d) -> p t d", t=T)
        ml_gate = work[:, 4096:6144].rearrange("p (t d) -> p t d", t=T)
        ml_scores = work[:, 6144:7680].rearrange("p (h n) -> p h n", n=QB)
        ml_decay = work[:, 7680:9216].rearrange("p (h n) -> p h n", n=QB)
        ml_bound = work[:, 9216:9600]
        ml_select = work[0:M_HEADS, 9600:10112]
        ML_ONES, ML_F, ML_G, ML_M, ML_FLOOR = [work[0:M_HEADS, c:c + S] for c in range(10112, 10112 + 5 * S, S)]
        ml_pre = ml_small[:, 0:16].rearrange("p (t n) -> p t n", t=T)
        ml_log = ml_small[:, 16:24].rearrange("p (t h) -> p t h", t=T)
        ml_cols = ml_small[:, 32:48].rearrange("p (c t h) -> p c t h", c=2, t=T)
        ml_moments = ml_small[:, 96:112].rearrange("p (h t c) -> p h t c", t=T, c=2)
        ml_inv, ml_var, ml_half, ml_rs, ml_scale = [
            ml_small[:, c:c + 8] for c in (112, 120, 128, 136, 144)]
        ml = {n: sem("mlstm_" + n) for n in (
            "consts", "bias_loaded", "o_kept", "gated", "biased", "tanh", "abs", "log", "gates_ready", "gates_turned",
            "m_ready", "floor_ready", "cols_turned", "spread", "cols_kept", "bounded", "decay_ready", "q_kept", "k_kept",
            "v_kept", "scores_ready", "weights_ready", "out_ready")}
        sin1 = trig[:, 0:32].rearrange("p (t n) -> p t n", t=T)
        sin2 = trig[:, 32:48].rearrange("p (t n) -> p t n", t=T)
        cos1 = trig[:, 48:80].rearrange("p (t n) -> p t n", t=T)
        cos2 = trig[:, 80:96].rearrange("p (t n) -> p t n", t=T)
        NMAX, SUMS, RECIP, SINKX, SMALL = range(5)

        ATT = ("rows_kept_a", "rows_kept_v", "roped", "k_copied", "fill_ready", "fill_a", "fill_v", "v_kept", "scores_ready",
               "max_ready", "probs_ready", "probs_turned", "probs_kept", "out_ready", "sum_read", "sink_exp",
               "squares", "c_rows", "c_turned", "c_high", "c_kept", "bias_used")
        mla_s = {n: sem("mla_" + n) for n in ATT}
        swa_s = {n: sem("swa_" + n) for n in ATT}
        p_loaded = sem("ple_rows_loaded")
        ple_s = {n: sem("ple_" + n) for n in ("turned", "high", "kept", "biased", "gate")}
        ple_rows = work[:, 12800:13312].rearrange("p (t n) -> p t n", t=T)

        def rope(E, order, rows, sin, cos, n):
            heads = rows.shape[2]
            shape = [P, T, heads, n]
            size = T * heads * n
            prods = [square_out[:, :, :].rearrange("p t d -> p (t d)")[:, j * size:(j + 1) * size]
                     .rearrange("p (t h n) -> p t h n", t=T, h=heads) for j in range(4)]
            x1, x2 = rows[:, :, :, 0:n], rows[:, :, :, n:2 * n]
            for t in range(T):
                c = cos[:, t, :].unsqueeze(1).broadcast_to([P, heads, n])
                s_ = sin[:, t, :].unsqueeze(1).broadcast_to([P, heads, n])
                for dst, src, by in ((0, x1, c), (1, x2, s_), (2, x2, c), (3, x1, s_)):
                    last = E.tensor_tensor(prods[dst][:, t], src[:, t], by, ALU.mult)
                    if not (t == T - 1 and dst == 3):
                        order.count(last)
            order.link(last)
            for t in range(T):
                last = E.tensor_tensor(x1[:, t], prods[0][:, t], prods[1][:, t], ALU.subtract)
                order.count(last)
                last = E.tensor_tensor(x2[:, t], prods[2][:, t], prods[3][:, t], ALU.add)
                if t < T - 1:
                    order.count(last)
            return last

        def diagonal(ap):
            return ap.rearrange("p (b n) -> p b n", n=P)[:, 0:3:2, :]

        @block.sync
        def _(sp):
            def load(u, i, src, k, n):
                if u >= RING:
                    sp.wait_ge(unit_ready, u - RING + 1 + LOOP_UNITS * i)
                sp.dma_start(slot(raw, u, k)[:, :, 0:n], src).then_inc(landed[u % RING], 16)

            def ffn(U, l, f):
                w_in, w_out = ffn_in[l][f], ffn_out[l][f]

                def step(r, i):
                    gate, up, down = ffn_units(U, r)
                    load(gate, i, w_in[r + FFN_BODY * i], 8, GW)
                    load(up, i, w_in[FG + r + FFN_BODY * i], 8, GW)
                    if r:
                        load(down, i, w_out[r - 1 + FFN_BODY * i], 2, D)

                for r in range(FFN_FIRST):
                    step(r, 0)
                with sp.Fori(0, FFN_TRIPS) as i:
                    for r in range(FFN_FIRST, FFN_FIRST + FFN_BODY):
                        step(r, i)
                load(U + 3 * FG - 1, 0, w_out[FG - 1], 2, D)

            def mlp(U, l):
                def step(r, i):
                    up, down = mlp_units(U, r)
                    load(up, i, mlp_up[l][r + MLP_BODY * i], 8, GW)
                    if r:
                        load(down, i, mlp_down[l][r - 1 + MLP_BODY * i], 2, D)

                for r in range(MLP_FIRST):
                    step(r, 0)
                with sp.Fori(0, MLP_TRIPS) as i:
                    for r in range(MLP_FIRST, MLP_FIRST + MLP_BODY):
                        step(r, i)
                load(U + 2 * MG - 1, 0, mlp_down[l][MG - 1], 2, D)

            def quarters(U, w, col=0, halves=2):
                w = quarter_units(w[:, col:col + halves * BANK])
                for c in range(halves):
                    for h in range(2):
                        load(U + 2 * c + h, 0, w[h, c], 4, BANK)

            def columns(U, w, col, n):
                w = col_units(w[:, col:col + n * GW])
                for j in range(n):
                    load(U + j, 0, w[j], 8, GW)

            sp.dma_start(x[:, :, :], x_d).then_inc(x_loaded, 16)
            sp.dma_start(gain_rows[0:12 * KD, :], g.rearrange("l n (k p) -> (l n k) p", p=P)).then_inc(gains_loaded, 16)
            sp.dma_start(gain_rows[12 * KD:12 * KD + 2, :],
                         a["mla_q_norm"].rearrange("l (k p) -> (l k) p", p=P)).then_inc(gains_loaded, 16)
            sp.dma_start(gain_rows[12 * KD + 2:NG, :], a["mla_kv_norm"]).then_inc(gains_loaded, 16)
            for t in range(2):
                sp.dma_start(pos_i[2 * t:2 * t + 2, :], a[("positions", "positions_2")[t]].rearrange(
                    "b (t p) -> (b t) p", p=P)).then_inc(pos_loaded, 16)
            for s, (name, U, n) in enumerate(plan):
                if name == "ffn":
                    ffn(U, n // 2, n % 2)
                if name == "sb":
                    w_in, w_out = a["sb_w_in"][0], a["sb_w_out"][0]
                    quarters(U, w_in, 2 * D)
                    columns(U + 4, w_in, 0, 8)
                    quarters(U + 12, w_out)
                if name == "mla":
                    w_in, w_uq, w_ukv = a["mla_w_in"][0], a["mla_w_uq"][0], a["mla_w_ukv"][0]
                    for h in range(2):
                        load(U + h, 0, w_in[h * BANK:(h + 1) * BANK, :].rearrange("(k p) n -> p k n", p=P), 4, MLA_IN)
                    w_uq = w_uq.rearrange("(k p) n -> p k n", p=P)
                    load(U + 2, 0, w_uq[:, :, 0:D], 2, D)
                    load(U + 3, 0, w_uq[:, :, D:D + BANK], 2, BANK)
                    load(U + 4, 0, w_ukv.rearrange("(k p) n -> p k n", p=P), 1, UNIT)
                    quarters(U + 5, a["mla_w_out"][0])
                if name == "mlstm":
                    w_in = a["a_w_in_2"][0]
                    quarters(U, w_in, 2 * D)
                    load(U + 4, 0, w_in[:, 3 * D:3 * D + 2 * M_HEADS].rearrange("(k p) n -> p k n", p=P), 8, 2 * M_HEADS)
                    quarters(U + 5, w_in, D)
                    columns(U + 9, w_in, 0, 4)
                    quarters(U + 13, a["a_w_out_2"][0])
                if name == "swa":
                    quarters(U, a["kv_w_2"], 0, 1)
                    quarters(U + 2, a["b_w_q_2"][0])
                    quarters(U + 6, a["b_w_o_2"][0])
                if name == "ple":
                    if s > 1:
                        sp.wait_ge(x_ready, T * (s - 1))
                    sp.dma_start(ple_rows, a["p_2"][n].rearrange("b (t p) n -> p (b t) n", p=P)).then_inc(p_loaded, 16)
                    load(U, 0, row_units(a["ple_w_proj_2"][n])[0], 2, D)
                    quarters(U + 1, a["ple_w_gate_2"][n])
                if name == "mlp":
                    mlp(U, n)
            sp.wait_ge(x_ready, T * len(STAGES))
            sp.dma_start(out_d, x[:, :, :]).then_inc(out_stored, 16)
            sp.wait_ge(out_stored, 16)

        @block.gpsimd
        def _(pool):
            nc.gpsimd.memset(ident[:, :], 0.0).then_inc(pool_chain, 1)
            pool.wait_ge(pool_chain, 1)
            nc.gpsimd.affine_select(out=ident[:, :], in_=ident[:, :], compare_op=ALU.not_equal, fill=1.0,
                                    base=0, pattern=[[-1, P]], channel_multiplier=1).then_inc(ident_ready, 1)
            nc.gpsimd.memset(neg_tri[:, :], -1.0).then_inc(pool_chain, 1)
            nc.gpsimd.memset(neg_ones[:, :], -1.0).then_inc(pool_chain, 1)
            nc.gpsimd.memset(later[:, :], 1.0).then_inc(pool_chain, 1)
            pool.wait_ge(pool_chain, 4)
            nc.gpsimd.affine_select(out=neg_tri[:, :], in_=neg_tri[:, :], compare_op=ALU.is_ge, fill=0.0,
                                    base=0, pattern=[[-1, P]], channel_multiplier=1).then_inc(masks_ready, 1)
            nc.gpsimd.affine_select(out=later[:, :], in_=later[:, :], compare_op=ALU.is_gt, fill=0.0,
                                    base=0, pattern=[[1, P]], channel_multiplier=-1).then_inc(masks_ready, 1)

            for col, theta, width in ((0, 10000.0, ROPE), (16, 500000.0, ROPE2)):
                for j, f in enumerate(inverse_frequencies(theta, width)):
                    ins = nc.gpsimd.memset(inv_freq[:, col + j:col + j + 1], float(f))
                    ins.then_inc(freq_ready, 1)
            for bias in (causal, window):
                nc.gpsimd.memset(bias[:, :], 0.0).then_inc(pool_chain, 1)
            pool.wait_ge(pool_chain, 6)
            for bias in (causal, window):
                d = diagonal(bias[:, :])
                nc.gpsimd.affine_select(out=d, in_=d, compare_op=ALU.is_ge, fill=MASKED, base=0,
                                        pattern=[[0, 2], [-1, P]], channel_multiplier=1).then_inc(bias_ready, 1)
            nc.gpsimd.affine_select(out=window[:, P:S], in_=window[:, P:S], compare_op=ALU.is_gt, fill=MASKED, base=0,
                                    pattern=[[1, P]], channel_multiplier=-1).then_inc(bias_ready, 1)
            for j, b in enumerate(("a_b_igate_2", "a_b_fgate_2")):
                pool.dma_start(gate_bias[:, j * M_HEADS:(j + 1) * M_HEADS],
                               a[b][0].partition_broadcast(P)).then_inc(ml["bias_loaded"], 16)
            pool.dma_start(sinks[:, :], a["b_sinks_2"][0].partition_broadcast(P)).then_inc(sinks_loaded, 16)

            def mla_stage():
                pool.wait_ge(trig_ready, 1)
                pool.wait_ge(mla_s["fill_a"], 1)
                pool.wait_ge(mla_s["fill_v"], 1)
                pool.wait_ge(mla_s["rows_kept_v"], 1)
                rope(nc.gpsimd, order, mla_q[:, :, :, NOPE:MLA_W], sin1, cos1, ROPE // 2).then_inc(mla_s["roped"], 1)
                pool.wait_ge(mla_s["roped"], 1)
                pool.wait_ge(mla_s["c_kept"], 4)
                nc.gpsimd.tensor_copy(mla_kT[NOPE:MLA_W, 1:HEADS, :],
                                      mla_kT[NOPE:MLA_W, 0:1, :].broadcast_to([ROPE, HEADS - 1, S]),
                                      ).then_inc(mla_s["k_copied"], 1)

            def mlstm_stage(s, nv):
                if s:
                    pool.wait_ge(x_ready, T * s)
                order.count(nc.gpsimd.memset(ml_bound, 0.0))
                order.link(nc.gpsimd.memset(ml_select, 0.0))
                d = diagonal(ml_bound)
                nc.gpsimd.affine_select(out=d, in_=d, compare_op=ALU.is_ge, fill=MASKED, base=0,
                                        pattern=[[0, 2], [1, P]], channel_multiplier=-1).then_inc(ml["consts"], 1)
                sel = ml_select.rearrange("p (h n) -> p h n", n=P)
                nc.gpsimd.affine_select(out=sel, in_=sel, compare_op=ALU.not_equal, fill=-1.0, base=0,
                                        pattern=[[-1, M_HEADS], [0, P]], channel_multiplier=1).then_inc(ml["consts"], 1)
                pool.wait_ge(vec_loaded[nv % 3], 16 * (nv // 3 + 1))
                for t in range(T):
                    pool.wait_ge(ml["o_kept"], t + 1)
                    nc.gpsimd.tensor_tensor(ml_gate[:, t, :], ml_gate[:, t, :], vec[:, nv % 3, :],
                                            ALU.mult).then_inc(ml["gated"], 1)

            def swa_stage():
                pool.wait_ge(trig_ready, 1)
                pool.wait_ge(swa_s["rows_kept_v"], 1)
                k = swa_kv[:, :, 0:KV_HEADS * HD].rearrange("p t (h w) -> p t h w", w=HD)
                rope(nc.gpsimd, order, k[:, :, :, 0:ROPE2], sin2, cos2, ROPE2 // 2).then_inc(swa_s["roped"], 1)
                pool.wait_ge(swa_s["roped"], 1)
                pool.wait_ge(swa_s["rows_kept_v"], 2)
                rope(nc.gpsimd, order, swa_q[:, :, :, 0:ROPE2], sin2, cos2, ROPE2 // 2).then_inc(swa_s["roped"], 1)

            def vectors(upto):
                while sent[0] < min(upto, len(VECTORS)):
                    n = sent[0]
                    if n >= 3:
                        _, s, j = VECTORS[n - 3]
                        if STAGES[s] == "swa" and j < 2:
                            pool.wait_ge(swa_s["rows_kept_v"], j + 1)
                        else:
                            pool.wait_ge(x_ready, T * (s + 1))
                    v = VECTORS[n][0]
                    pool.dma_start(vec[:, n % 3, 0:v.shape[0]], v.partition_broadcast(P)).then_inc(vec_loaded[n % 3], 16)
                    sent[0] += 1

            def sb_stage():
                for h in range(HEADS):
                    pool.wait_ge(sbs["raw_ready"], h + 1)
                    d = diagonal(sb_a[:, h % 2, :])
                    nc.gpsimd.affine_select(out=d, in_=d, compare_op=ALU.is_gt, fill=0.0, base=0,
                                            pattern=[[0, 2], [1, P]], channel_multiplier=-1,
                                            ).then_inc(sbs["weights_ready"], 1)

            order = Chain(pool, pool_order)
            sent, used = [0], 0
            for s, (name, U, n) in enumerate(plan):
                vectors(used + 3)
                if name == "sb":
                    sb_stage()
                if name == "mla":
                    mla_stage()
                if name == "mlstm":
                    mlstm_stage(s, used)
                if name == "swa":
                    swa_stage()
                    vectors(used + 5)
                used += VECTORS_USED[name]

        @block.tensor
        def _(pe):
            def wait_unit(u, i=0):
                pe.wait_ge(unit_ready, u + 1 + LOOP_UNITS * i)

            def product(dst, left, right, first, last):
                (lh, ll), (rh, rl) = left, right
                nc.tensor.matmul(dst, lh, rh, start=first, stop=False)
                nc.tensor.matmul(dst, lh, rl, start=False, stop=False)
                return nc.tensor.matmul(dst, ll, rh, start=False, stop=last)

            def turn(m, src, ready):
                for t in range(T):
                    pe.wait_ge(*ready(t))
                    for k in range(KD):
                        mm = nc.tensor.transpose(wk[:, k // 2, (k % 2) * S + t * P:(k % 2) * S + (t + 1) * P],
                                                 src[:, t, k * P:(k + 1) * P], ident[:, :])
                        if t == T - 1 and k % 2:
                            mm.then_inc(turned, 1)
                pe.wait_ge(turned_kept, KD // 2 * (m + 1))

            def group_up(u, i, bank):
                wait_unit(u, i)
                wh, wl = slot(whi, u, 8), slot(wlo, u, 8)
                for h in range(2):
                    c = slice(h * P, (h + 1) * P)
                    for k in range(KD):
                        mm = product(wk[:, bank, h * S:(h + 1) * S], (wh[:, k, c], wl[:, k, c]),
                                     (xTh[:, k, :], xTl[:, k, :]), k == 0, k == KD - 1)
                mm.then_inc(unit_done, 1)

            def group_down(u, i, b, first, last):
                wait_unit(u, i)
                wh, wl = slot(whi, u, 2), slot(wlo, u, 2)
                for k in range(2):
                    for t in range(T):
                        r = slice(t * P, (t + 1) * P)
                        for c in range(2):
                            n = slice(c * BANK, (c + 1) * BANK)
                            mm = product(acc[:, t, n], (hTh[:, b, k, r], hTl[:, b, k, r]),
                                         (wh[:, k, n], wl[:, k, n]), first and k == 0, last and k == 1)
                mm.then_inc(unit_done, 1)

            def row_product(U, dst, halves=2, n=BANK):
                for c in range(halves):
                    for h in range(2):
                        u = U + 2 * c + h
                        wait_unit(u)
                        wh, wl = slot(whi, u, 4), slot(wlo, u, 4)
                        for k in range(4):
                            for t in range(T):
                                r = slice(t * P, (t + 1) * P)
                                mm = product(dst(t, c), (xTh[:, 4 * h + k, r], xTl[:, 4 * h + k, r]),
                                             (wh[:, k, 0:n], wl[:, k, 0:n]), h == 0 and k == 0, h == 1 and k == 3)
                        mm.then_inc(unit_done, 1)

            def ffn(U, H):
                def up(r, i):
                    gate, up, _ = ffn_units(U, r)
                    group_up(gate, i, 2 * (r % 2))
                    group_up(up, i, 2 * (r % 2) + 1)

                def down(r, i):
                    pe.wait_ge(hidden_ready, H + r + 1 + FFN_BODY * i)
                    u = ffn_units(U, r + 1)[2] if r < FG - 1 else U + 3 * FG - 1
                    group_down(u, i, r % 2, r == 0, r == FG - 1)

                up(0, 0)
                for r in range(1, FFN_FIRST):
                    up(r, 0)
                    down(r - 1, 0)
                with pe.Fori(0, FFN_TRIPS) as i:
                    for r in range(FFN_FIRST, FFN_FIRST + FFN_BODY):
                        up(r, i)
                        down(r - 1, i)
                down(FG - 1, 0)

            def mlp(U, H):
                def up(r, i):
                    group_up(mlp_units(U, r)[0], i, r % 3)

                def down(r, i):
                    pe.wait_ge(hidden_ready, H + r + 1 + MLP_BODY * i)
                    u = mlp_units(U, r + 1)[1] if r < MG - 1 else U + 2 * MG - 1
                    group_down(u, i, r % 3, r == 0, r == MG - 1)

                up(0, 0)
                for r in range(1, MLP_FIRST):
                    up(r, 0)
                    down(r - 1, 0)
                with pe.Fori(0, MLP_TRIPS) as i:
                    for r in range(MLP_FIRST, MLP_FIRST + MLP_BODY):
                        up(r, i)
                        down(r - 1, i)
                down(MG - 1, 0)

            def sb_stage(U):
                row_product(U, lambda t, c: acc[:, t, c * BANK:(c + 1) * BANK])
                for j in range(8):
                    if j >= 4:
                        pe.wait_ge(sbs["q_kept"], j - 3)
                    group_up(U + 4 + j, 0, j % 4)
                pe.wait_ge(sbs["k_kept"], 4)
                pe.wait_ge(sbs["v_kept"], 1)
                pe.wait_ge(masks_ready, 2)

                def scores(h):
                    r = slice(HD * (h % 2), HD * (h % 2) + HD)
                    z, q, k = wk[:, h % 4, :], sb_q[r, h // 2, :], sb_k[r, h // 2, :]
                    nc.tensor.matmul(z[:, 0:S], k[:, 0:P], q, start=True, stop=False, skip_group_check=True)
                    nc.tensor.matmul(z[:, S:QB], k[:, P:S], q[:, P:S], start=False, stop=False,
                                     skip_group_check=True).then_inc(sbs["z_ready"], 1)

                def tails(h):
                    pe.wait_ge(sbs["softplus_ready"], h + 1)
                    z, sp = wk[:, h % 4, :], hid[:, h % 3, :]
                    nc.tensor.matmul(z[:, 0:S], neg_tri[:, :], sp[:, 0:S], start=False, stop=False, skip_group_check=True)
                    nc.tensor.matmul(z[:, P:S], neg_ones[:, :], sp[:, S:QB], start=False, stop=False, skip_group_check=True)
                    nc.tensor.matmul(z[:, S:QB], neg_tri[:, :], sp[:, S:QB], start=False, stop=True,
                                     skip_group_check=True).then_inc(sbs["logits_ready"], 1)

                def values(h):
                    j, b = h // 2, HD * (h % 2)
                    pe.wait_ge(sbs["weights_ready"], h + 1)
                    if j >= 2 and h % 2 == 0:
                        pe.wait_ge(sbs["out_kept"], j - 1)
                    o, w = acc[b:b + HD, j % 2, :], sb_a[:, h % 2, :]
                    nc.tensor.matmul(o[:, 0:S], sb_v[:, 0, h * HD:(h + 1) * HD], w[:, 0:S], start=True, stop=False,
                                     skip_group_check=True)
                    nc.tensor.matmul(o[:, P:S], sb_v[:, 1, h * HD:(h + 1) * HD], w[:, S:QB], start=False, stop=True,
                                     skip_group_check=True).then_inc(sbs["out_ready"], 1)

                scores(0)
                scores(1)
                for h in range(HEADS):
                    if h + 2 < HEADS:
                        scores(h + 2)
                    tails(h)
                    if h:
                        values(h - 1)
                values(HEADS - 1)
                pe.wait_ge(sbs["out_kept"], PAIRS)
                row_product(U + 12, lambda t, c: acc[:, t, c * BANK:(c + 1) * BANK])

            def attention(sm, qT, kT, v):

                def scores(h):
                    s = wk[:, h % 2, :]
                    if h >= 2:
                        pe.wait_ge(sm["max_ready"], h - 1)
                    nc.tensor.matmul(s[:, 0:P], qT[:, h, 0:P], kT(h)[:, 0:P], start=True, stop=True)
                    nc.tensor.matmul(s[:, P:QB], qT[:, h, P:S], kT(h), start=True, stop=True).then_inc(sm["scores_ready"], 1)

                def turn_probs(h):
                    pe.wait_ge(sm["probs_ready"], h + 1)
                    if h >= 2:
                        pe.wait_ge(sm["probs_kept"], h - 1)
                    for b in range(3):
                        mm = nc.tensor.transpose(wk[:, 2 + h % 2, b * P:(b + 1) * P], hid[:, h % 3, b * P:(b + 1) * P],
                                                 ident[:, :])
                    mm.then_inc(sm["probs_turned"], 1)

                def values(h):
                    pe.wait_ge(sm["probs_kept"], h + 1)
                    c = slice(h * HD, (h + 1) * HD)
                    p = probs_T[:, h % 2, :]
                    nc.tensor.matmul(acc[:, 0, c], p[:, 0:P], v(h, 0), start=True, stop=True)
                    nc.tensor.matmul(acc[:, 1, c], p[:, P:S], v(h, 0), start=True, stop=False)
                    nc.tensor.matmul(acc[:, 1, c], p[:, S:QB], v(h, 1), start=False, stop=True).then_inc(sm["out_ready"], 1)

                scores(0)
                scores(1)
                for h in range(HEADS):
                    if h + 2 < HEADS:
                        scores(h + 2)
                    turn_probs(h)
                    if h:
                        values(h - 1)
                values(HEADS - 1)

            def fill_free(sm, f):
                if f >= 4:
                    kept = (f - 4) // 2 + 1
                    pe.wait_ge(sm["fill_a" if f % 2 == 0 else "fill_v"], kept)

            def mla_stage(U):
                for h in range(2):
                    wait_unit(U + h)
                    wh, wl = slot(whi, U + h, 4), slot(wlo, U + h, 4)
                    for k in range(4):
                        for t in range(T):
                            r = slice(t * P, (t + 1) * P)
                            mm = product(acc[:, t, 0:MLA_IN], (xTh[:, 4 * h + k, r], xTl[:, 4 * h + k, r]),
                                         (wh[:, k, 0:MLA_IN], wl[:, k, 0:MLA_IN]), h == 0 and k == 0, h == 1 and k == 3)
                    mm.then_inc(unit_done, 1)
                pe.wait_ge(mla_s["c_rows"], 1)
                for bank, col, width in ((0, 0, P), (0, P, P), (1, 2 * P, P), (2, 3 * P, MLA_W)):
                    for t in range(T):
                        at = S if (bank == 0 and col) else 0
                        mm = nc.tensor.transpose(wk[0:width, bank, at + t * P:at + (t + 1) * P],
                                                 xn[:, t, col:col + width], ident[:, :])
                    mm.then_inc(mla_s["c_turned"], 1)
                pe.wait_ge(mla_s["c_kept"], 4)
                wait_unit(U + 2)
                for u, dst, base in ((U + 2, lambda t, c: acc[:, t, c * BANK:(c + 1) * BANK], 2), (U + 3, lambda t, c: wk[:, t, :], 1)):
                    wait_unit(u)
                    wh, wl = slot(whi, u, 2), slot(wlo, u, 2)
                    for k in range(2):
                        for t in range(T):
                            r = slice(t * P, (t + 1) * P)
                            for c in range(base):
                                n = slice(c * BANK, (c + 1) * BANK)
                                mm = product(dst(t, c), (xTh[:, k, r], xTl[:, k, r]), (wh[:, k, n], wl[:, k, n]), k == 0, k == 1)
                    mm.then_inc(unit_done, 1)
                u = U + 4
                wait_unit(u)
                wh, wl = whi[:, u % RING, :], wlo[:, u % RING, :]
                for j in range(PAIRS):
                    f = 2 + j
                    fill_free(mla_s, f)
                    for e in range(2):
                        c = slice((2 * j + e) * P, (2 * j + e + 1) * P)
                        mm = product(wk[:, f % 4, e * S:(e + 1) * S], (wh[:, c], wl[:, c]), (xTh[:, 2, :], xTl[:, 2, :]), True, True)
                    mm.then_inc(mla_s["fill_ready"], 1)
                pe.wait_ge(mla_s["rows_kept_v"], 1)
                wh, wl = slot(whi, u, HEADS), slot(wlo, u, HEADS)
                for t in range(T):
                    r = slice(t * P, (t + 1) * P)
                    for c in range(2):
                        h = slice(8 * c, 8 * c + 8)
                        mm = product(acc[:, t, c * BANK:(c + 1) * BANK], (xTh[:, 2, r], xTl[:, 2, r]),
                                     (wh[:, h, NOPE:P], wl[:, h, NOPE:P]), True, True)
                mm.then_inc(unit_done, 1)
                pe.wait_ge(mla_s["roped"], 1)
                turn_heads(mla_s, 10, mla_q, HEADS, MLA_W)
                pe.wait_ge(mla_s["fill_a"], 9)
                pe.wait_ge(mla_s["fill_v"], 9)
                pe.wait_ge(mla_s["k_copied"], 1)
                pe.wait_ge(mla_s["v_kept"], 1)
                attention(mla_s, mla_qT, lambda h: mla_kT[:, h, :], lambda h, t: mla_v[:, t, h * HD:(h + 1) * HD])

            def turn_heads(sm, f0, rows, heads, width, shift=0):
                for j in range(heads // 2):
                    f = f0 + j
                    fill_free(sm, f)
                    for e in range(2):
                        for t in range(T):
                            mm = nc.tensor.transpose(wk[0:width, (f + shift) % 4, e * S + t * P:e * S + (t + 1) * P],
                                                     rows[:, t, 2 * j + e, :], ident[:, :])
                    mm.then_inc(sm["fill_ready"], 1)

            def mlstm_stage(U):
                row_product(U, lambda t, c: acc[:, t, c * BANK:(c + 1) * BANK])
                u = U + 4
                wait_unit(u)
                wh, wl = slot(whi, u, 8), slot(wlo, u, 8)
                for t in range(T):
                    r = slice(t * P, (t + 1) * P)
                    for k in range(KD):
                        mm = product(wk[:, 0, t * 8:t * 8 + 8], (xTh[:, k, r], xTl[:, k, r]),
                                     (wh[:, k, 0:8], wl[:, k, 0:8]), k == 0, k == KD - 1)
                mm.then_inc(unit_done, 1)
                pe.wait_ge(ml["o_kept"], T)
                row_product(U + 5, lambda t, c: acc[:, t, 0:BANK], halves=1)
                pe.wait_ge(ml["gates_ready"], 1)
                for j in range(2):
                    for t in range(T):
                        mm = nc.tensor.transpose(wk[0:M_HEADS, 1, j * S + t * P:j * S + (t + 1) * P],
                                                 ml_pre[:, t, j * M_HEADS:(j + 1) * M_HEADS], ident[:, :])
                mm.then_inc(ml["gates_turned"], 1)
                row_product(U + 7, lambda t, c: acc[:, t, BANK:D], halves=1)
                pe.wait_ge(ml["consts"], 2)
                pe.wait_ge(ml["m_ready"], 1)
                pe.wait_ge(ml["floor_ready"], 1)
                for j, rows in enumerate((ML_G, ML_FLOOR)):
                    for t in range(T):
                        mm = nc.tensor.transpose(wk[:, 2, 8 * j + 4 * t:8 * j + 4 * t + 4], rows[:, t * P:(t + 1) * P],
                                                 ident[0:M_HEADS, 0:M_HEADS])
                mm.then_inc(ml["cols_turned"], 1)
                for h in range(M_HEADS):
                    mm = nc.tensor.matmul(wk[:, (3, 0)[h // 2], (h % 2) * S:(h % 2 + 1) * S],
                                          ml_select[:, h * P:(h + 1) * P], ML_M, start=True, stop=True)
                    if h % 2:
                        mm.then_inc(ml["spread"], 1)
                for j, bank in enumerate((1, 2, 3, 0)):
                    if j == 1:
                        pe.wait_ge(ml["cols_kept"], 1)
                    if j >= 2:
                        pe.wait_ge(ml["bounded"], 2 * (j - 1))
                    group_up(U + 9 + j, 0, bank)
                pe.wait_ge(ml["q_kept"], 2)
                pe.wait_ge(ml["k_kept"], 2)

                def scores(h):
                    z, q, k = wk[:, h, :], ml_q[:, h, :], ml_k[:, h, :]
                    nc.tensor.matmul(z[:, 0:S], k[:, 0:P], q, start=True, stop=True)
                    nc.tensor.matmul(z[:, S:QB], k[:, P:S], q[:, P:S], start=True, stop=True).then_inc(ml["scores_ready"], 1)

                def outputs(h):
                    pe.wait_ge(ml["weights_ready"], h + 1)
                    w = ml_scores[:, h, :]
                    for rhs, dst in ((lambda t: ml_v[:, t, h * M_DV:(h + 1) * M_DV], lambda t: acc[:, t, h * M_DV:(h + 1) * M_DV]),
                                     (lambda t: neg_ones[:, 0:1], lambda t: wk[:, h, QB + t:QB + t + 1])):
                        nc.tensor.matmul(dst(0), w[:, 0:P], rhs(0), start=True, stop=True)
                        nc.tensor.matmul(dst(1), w[:, P:S], rhs(0), start=True, stop=False)
                        mm = nc.tensor.matmul(dst(1), w[:, S:QB], rhs(1), start=False, stop=True)
                    mm.then_inc(ml["out_ready"], 1)

                for h in range(M_HEADS):
                    scores(h)
                pe.wait_ge(ml["v_kept"], 1)
                for h in range(M_HEADS):
                    outputs(h)

            def swa_stage(U):
                row_product(U, lambda t, c: wk[:, t, :], halves=1)
                row_product(U + 2, lambda t, c: acc[:, t, c * BANK:(c + 1) * BANK])
                k = swa_kv[:, :, 0:KV_HEADS * HD].rearrange("p t (h w) -> p t h w", w=HD)
                pe.wait_ge(swa_s["roped"], 1)
                turn_heads(swa_s, 0, k, KV_HEADS, HD, 2)
                pe.wait_ge(swa_s["roped"], 2)
                turn_heads(swa_s, 2, swa_q, HEADS, HD, 2)
                pe.wait_ge(swa_s["fill_a"], 5)
                pe.wait_ge(swa_s["fill_v"], 5)
                group = HEADS // KV_HEADS
                attention(swa_s, swa_qT, lambda h: swa_kT[:, h // group, :],
                          lambda h, t: swa_kv[:, t, (KV_HEADS + h // group) * HD:(KV_HEADS + h // group + 1) * HD])

            def ple_stage(U, n, m, s):
                pe.wait_ge(p_loaded, 16 * (n + 1))
                for k in range(2):
                    for t in range(T):
                        mm = nc.tensor.transpose(wk[:, 0, k * S + t * P:k * S + (t + 1) * P],
                                                 ple_rows[:, t, k * P:(k + 1) * P], ident[:, :])
                mm.then_inc(ple_s["turned"], 1)
                pe.wait_ge(ple_s["kept"], n + 1)
                turn(m, x, lambda t: (x_ready, T * s - 1 + t))
                u = U
                wait_unit(u)
                wh, wl = slot(whi, u, 2), slot(wlo, u, 2)
                for k in range(2):
                    for t in range(T):
                        r = slice(t * P, (t + 1) * P)
                        for c in range(2):
                            q = slice(c * BANK, (c + 1) * BANK)
                            mm = product(wk[:, 2 * t + c, :], (hTh[:, 0, k, r], hTl[:, 0, k, r]),
                                         (wh[:, k, q], wl[:, k, q]), k == 0, k == 1)
                mm.then_inc(unit_done, 1)
                row_product(U + 1, lambda t, c: acc[:, t, c * BANK:(c + 1) * BANK])

            pe.wait_ge(ident_ready, 1)
            pe.wait_ge(gains_loaded, 48)
            nc.tensor.transpose(wk[:, 3, 0:NG], gain_rows[:, :], ident[0:NG, 0:NG]).then_inc(gains_turned, 1)
            pe.wait_ge(pos_made, 1)
            nc.tensor.transpose(wk[:, 2, 0:4], pos_rows[:, :], ident[0:4, 0:4]).then_inc(pos_turned, 1)
            pe.wait_ge(gains_kept, 1)
            pe.wait_ge(angles_ready, 1)
            m = rows = hidden = outs = 0
            for s, (name, U, n) in enumerate(plan):
                if name in ("ffn", "sb", "mla"):
                    turn(m, xn, lambda t: ((rows_v, rows_a)[t], rows + 1))
                    m, rows = m + 1, rows + 1
                if name == "ffn":
                    ffn(U, hidden)
                    hidden += FG
                if name == "sb":
                    sb_stage(U)
                if name == "mla":
                    mla_stage(U)
                if name in ("mlstm", "mlp", "swa"):
                    turn(m, x, lambda t: (x_ready, T * s - 1 + t))
                    m += 1
                if name == "mlp":
                    mlp(U, hidden)
                    hidden += MG
                if name == "mlstm":
                    mlstm_stage(U)
                if name == "swa":
                    swa_stage(U)
                if name == "ple":
                    ple_stage(U, n, m, s)
                    m += 1
                if name in ("mla", "mlstm", "swa"):
                    turn(m, xn, lambda t: (mixed, T * outs + t + 1))
                    m, outs = m + 1, outs + 1
                    row_product(U + STAGE_UNITS[name] - 4, lambda t, c: acc[:, t, c * BANK:(c + 1) * BANK])

        @block.scalar
        def _(act):
            chain = Chain(act, act_chain)
            A = nc.scalar.activation
            next_unit = [0]

            def split(u, i=0):
                act.wait_ge(landed[u % RING], 16 * (u // RING + 1) + 16 * (LOOP_UNITS // RING) * i)
                if u >= RING:
                    act.wait_ge(unit_done, u - RING + 1 + LOOP_UNITS * i)
                A(whi[:, u % RING, :], raw[:, u % RING, :], ACT.Copy).then_inc(high_ready, 1)

            def split_to(u):
                while next_unit[0] < min(u, TOTAL):
                    split(next_unit[0])
                    next_unit[0] += 1

            def sum_squares(src, t):
                A(square_out[:, t, :], src, ACT.Square, accum_out=stat[:, t:t + 1]).then_inc(squares_ready, 1)

            def keep_turned(m, gain):
                for b in range(KD // 2):
                    act.wait_ge(turned, KD // 2 * m + b + 1)
                    if gain is None:
                        A(xTh[:, 2 * b:2 * b + 2, :].rearrange("p k s -> p (k s)"), wk[:, b, :],
                          ACT.Copy).then_inc(turned_high, 1)
                    else:
                        for k in (2 * b, 2 * b + 1):
                            ins = A(xTh[:, k, :], wk[:, b, (k % 2) * S:(k % 2 + 1) * S], ACT.Copy,
                                    scale=gain[:, k:k + 1])
                        ins.then_inc(turned_high, 1)

            def rms_in(s, scales, rows, m, U, gain):
                for t in range(T):
                    if s == 0 and t == 0:
                        act.wait_ge(x_loaded, 16)
                    elif s:
                        act.wait_ge(x_ready, T * s - 1 + t)
                    sum_squares(x[:, t, :], t)
                act.wait_ge(scale_ready, scales + 1)
                A(xn[:, 1, :], x[:, 1, :], ACT.Copy, scale=stat[:, 9:10]).then_inc(rows_a, 1)
                split_to(U + RING)
                keep_turned(m, gain)

            def hidden_step(H, r, i, body, bank, buffer, func, gate, up, down):
                h = H + r
                act.wait_ge(unit_done, gate + 1 + LOOP_UNITS * i)
                back = body if body == 3 else 2
                if h - back + 1 > 0:
                    act.wait_ge(hidden_ready, h - back + 1 + body * i)
                A(hid[:, buffer, :], wk[:, bank, :], func).then_inc(act_ready, 1)
                split(gate + 3, i)
                if up is not None:
                    split(up + 3, i)
                act.wait_ge(hidden_made, h + 1 + body * i)
                A(hTh[:, buffer].rearrange("p k s -> p (k s)"), hid[:, buffer, :], ACT.Copy).then_inc(hidden_high, 1)
                if down is not None:
                    split(down + 3, i)

            def ffn(U, H):
                def step(r, i):
                    gate, up, down = ffn_units(U, r)
                    hidden_step(H, r, i, FFN_BODY, 2 * (r % 2), r % 2, ACT.Silu, gate, up, down if r else None)
                split_to(U + RING)
                for r in range(FFN_FIRST):
                    step(r, 0)
                with act.Fori(0, FFN_TRIPS) as i:
                    for r in range(FFN_FIRST, FFN_FIRST + FFN_BODY):
                        step(r, i)
                next_unit[0] = U + 3 * FG + 2

            def mlp(U, H):
                def step(r, i):
                    up, down = mlp_units(U, r)
                    hidden_step(H, r, i, MLP_BODY, r % 3, r % 3, ACT.Relu, up, None, down if r else None)
                split_to(U + RING)
                for r in range(MLP_FIRST):
                    step(r, 0)
                with act.Fori(0, MLP_TRIPS) as i:
                    for r in range(MLP_FIRST, MLP_FIRST + MLP_BODY):
                        step(r, i)
                next_unit[0] = U + 2 * MG + 2

            def sb_stage(U):
                for j in range(12):
                    if j >= 8:
                        act.wait_ge(unit_done, U + j + 1)
                        A(sb_k[:, 2 * (j - 8):2 * (j - 7), :].rearrange("p j s -> p (j s)"), wk[:, j - 8, :],
                          ACT.Copy).then_inc(sbs["k_kept"], 1)
                    split_to(U + RING + j + 1)

                def logs(h):
                    act.wait_ge(sbs["abs_ready"], h + 1)
                    e = hid[:, h % 3, 0:QB]
                    chain.link(A(e, e, ACT.Exp, scale=-1.0))
                    A(e, e, ACT.Ln, bias=1.0).then_inc(sbs["log_ready"], 1)

                act.preload_act_table_set("natural_log_exp_and_others")
                logs(0)
                logs(1)
                for h in range(HEADS):
                    if h + 2 < HEADS:
                        logs(h + 2)
                    act.wait_ge(sbs["logits_ready"], h + 1)
                    if h >= 2:
                        act.wait_ge(sbs["out_ready"], h - 1)
                    A(sb_a[:, h % 2, :], wk[:, h % 4, 0:QB], ACT.Exp).then_inc(sbs["raw_ready"], 1)
                    if h % 2 == 0 and h:
                        pair_high(h // 2 - 1)
                pair_high(PAIRS - 1)
                act.wait_ge(unit_done, U + 13)
                split_to(U + 16)

            def pair_high(j):
                act.wait_ge(sbs["out_ready"], 2 * j + 2)
                A(xTh[:, j, :], acc[:, j % 2, 0:S], ACT.Copy).then_inc(sbs["out_high"], 1)

            def keep_fills(sm, fills, first, dst, width, shift=0):
                for f in fills:
                    if f % 2 == 0:
                        act.wait_ge(sm["fill_ready"], f - first + 1)
                        j = f - fills[0]
                        A(dst[0:width, 2 * j:2 * j + 2, :], wk[0:width, (f + shift) % 4, :].rearrange(
                            "p (e s) -> p e s", e=2), ACT.Copy).then_inc(sm["fill_a"], 1)

            def attention(sm, sink):
                def keep_probs(h):
                    act.wait_ge(sm["probs_turned"], h + 1)
                    if h >= 2:
                        act.wait_ge(sm["out_ready"], h - 1)
                    A(probs_T[:, h % 2, :], wk[:, 2 + h % 2, 0:QB], ACT.Copy).then_inc(sm["probs_kept"], 1)

                act.preload_act_table_set("natural_log_exp_and_others")
                for h in range(HEADS):
                    act.wait_ge(sm["max_ready"], h + 1)
                    for t, c in ((0, slice(0, P)), (1, slice(P, QB))):
                        e, at = hid[:, h % 3, c], 2 * h + t
                        ins = A(e, e, ACT.Exp, bias=att_stat[:, NMAX, at:at + 1], accum_out=att_stat[:, SUMS, at:at + 1])
                    ins.then_inc(sm["probs_ready"], 1)
                    if h:
                        keep_probs(h - 1)
                    if sink and h in (8, HEADS - 1):
                        c = slice(0, HEADS) if h == 8 else slice(HEADS, 2 * HEADS)
                        act.wait_ge(sm["sum_read"], (h + 1) // 8)
                        A(att_stat[:, SMALL, c], att_stat[:, SINKX, c], ACT.Exp).then_inc(sm["sink_exp"], 1)
                keep_probs(HEADS - 1)

            def mla_stage(U):
                split_to(U + 4)
                act.wait_ge(unit_done, U + 2)
                for j, (t, c) in enumerate([(t, c) for c in (slice(0, Q_LORA), slice(Q_LORA, Q_LORA + KV_LORA)) for t in range(T)]):
                    A(square_out[:, t, c], acc[:, t, c], ACT.Square,
                      accum_out=stat[:, 16 + j:17 + j]).then_inc(mla_s["squares"], 1)
                split_to(U + 5)
                act.wait_ge(mla_s["c_turned"], 2)
                A(xTh[:, 0, :], wk[:, 0, 0:S], ACT.Copy, scale=gain_cols[:, 96:97])
                A(xTh[:, 1, :], wk[:, 0, S:2 * S], ACT.Copy, scale=gain_cols[:, 97:98]).then_inc(mla_s["c_high"], 1)
                act.wait_ge(mla_s["c_turned"], 3)
                A(xTh[:, 2, :], wk[:, 1, 0:S], ACT.Copy, scale=gain_cols[:, 98:99]).then_inc(mla_s["c_high"], 1)
                act.wait_ge(unit_done, U + 4)
                A(work[:, D:D + BANK], wk[:, 0, :], ACT.Copy).then_inc(mla_s["fill_a"], 1)
                split_to(U + 7)
                keep_fills(mla_s, range(2, 10), 2, mla_kT, NOPE)
                split_to(U + 8)
                keep_fills(mla_s, range(10, 18), 2, mla_qT, MLA_W)
                attention(mla_s, False)

            def mlstm_stage(U):
                split_to(U + 7)
                act.wait_ge(unit_done, U + 4)
                for t in range(T):
                    A(ml_gate[:, t, :], acc[:, t, :], ACT.Sigmoid).then_inc(ml["o_kept"], 1)
                split_to(U + 8)
                act.wait_ge(ml["biased"], 1)
                A(ml_small[:, 0:16], ml_small[:, 0:16], ACT.Tanh, scale=1.0 / GATE_CAP).then_inc(ml["tanh"], 1)
                act.wait_ge(ml["abs"], 1)
                act.preload_act_table_set("natural_log_exp_and_others")
                chain.link(A(ml_small[:, 16:24], ml_small[:, 16:24], ACT.Exp, scale=-1.0))
                A(ml_small[:, 16:24], ml_small[:, 16:24], ACT.Ln, bias=1.0).then_inc(ml["log"], 1)
                split_to(U + 10)
                act.wait_ge(ml["m_ready"], 1)
                A(ML_FLOOR, ML_FLOOR, ACT.Exp, scale=-1.0).then_inc(ml["floor_ready"], 1)
                split_to(U + 12)
                for h in range(M_HEADS):
                    act.wait_ge(ml["bounded"], h + 1)
                    A(ml_decay[:, h, :], ml_decay[:, h, :], ACT.Exp).then_inc(ml["decay_ready"], 1)
                split_to(U + 13)
                for j in range(2):
                    act.wait_ge(unit_done, U + 10 + j)
                    A(ml_q[:, 2 * j:2 * j + 2, :].rearrange("p h s -> p (h s)"), wk[:, 1 + j, :], ACT.Copy,
                      scale=M_DK ** -0.5).then_inc(ml["q_kept"], 1)
                    split_to(U + 14 + j)
                split_to(U + 16)

            def swa_stage(U):
                split_to(U + 9)
                keep_fills(swa_s, range(0, 2), 0, swa_kT, HD, 2)
                keep_fills(swa_s, range(2, 10), 0, swa_qT, HD, 2)
                attention(swa_s, True)

            def ple_stage(U, n, m):
                act.wait_ge(ple_s["turned"], n + 1)
                A(hTh[:, 0].rearrange("p k s -> p (k s)"), wk[:, 0, :], ACT.Copy).then_inc(ple_s["high"], 1)
                split_to(U + RING)
                keep_turned(m, None)
                split_to(U + 7)
                for t in range(T):
                    act.wait_ge(ple_s["biased"], T * n + t + 1)
                    A(xn[:, t, :], xn[:, t, :], ACT.Sigmoid).then_inc(ple_s["gate"], 1)

            act.wait_ge(angles_ready, 1)
            A(trig[:, :], angle[:, :], ACT.Sin).then_inc(trig_ready, 1)
            act.wait_ge(gains_kept, 1)
            m = rows = hidden = scales = 0
            for s, (name, U, n) in enumerate(plan):
                if name in ("ffn", "sb", "mla"):
                    col = {"ffn": (6 * (n // 2) + 4 * (n % 2)), "sb": 2, "mla": 8}[name] * KD
                    rms_in(s, scales, rows, m, U, gain_cols[:, col:col + KD])
                    m, rows, scales = m + 1, rows + 1, scales + 1
                if name == "ffn":
                    ffn(U, hidden)
                    hidden += FG
                if name == "sb":
                    sb_stage(U)
                if name == "mla":
                    mla_stage(U)
                if name in ("mlstm", "mlp", "swa"):
                    split_to(U + RING)
                    keep_turned(m, None)
                    m += 1
                if name == "mlp":
                    mlp(U, hidden)
                    hidden += MG
                if name == "mlstm":
                    mlstm_stage(U)
                if name == "swa":
                    swa_stage(U)
                if name == "ple":
                    ple_stage(U, n, m)
                    m += 1
                if name in ("mla", "mlstm", "swa"):
                    keep_turned(m, None)
                    m += 1
                    split_to(U + STAGE_UNITS[name] + 2)
                if name in ("ffn", "sb", "mla"):
                    act.wait_ge(unit_done, U + STAGE_UNITS[name])
                    for t in range(T):
                        sum_squares(acc[:, t, :], t)
                    scales += 1

        @block.vector
        def _(dve):
            chain = Chain(dve, dve_chain)
            V = nc.vector
            next_unit = [0]

            def split(u, i=0):
                dve.wait_ge(high_ready, u + 1 + LOOP_UNITS * i)
                V.tensor_tensor(wlo[:, u % RING, :], raw[:, u % RING, :], whi[:, u % RING, :].bitcast(F32),
                                ALU.subtract).then_inc(unit_ready, 1)

            def split_to(u):
                while next_unit[0] < min(u, TOTAL):
                    split(next_unit[0])
                    next_unit[0] += 1

            def rsqrt(var, half, y, weight=1.0):
                yi = y.bitcast(I32)
                chain.link(V.tensor_scalar(yi, var.bitcast(I32), 1, None, ALU.logical_shift_right))
                chain.link(V.tensor_scalar(yi, yi, -1.0, float(0x5f3759df), ALU.mult, ALU.add))
                for step in range(3):
                    chain.link(V.scalar_tensor_tensor(half, y, -0.5, y, ALU.mult, ALU.mult))
                    chain.link(V.tensor_tensor(half, half, var, ALU.mult))
                    last = V.scalar_tensor_tensor(y, half, 1.5, y, ALU.add, ALU.mult)
                    if step < 2 or weight != 1.0:
                        chain.link(last)
                if weight != 1.0:
                    last = V.tensor_scalar(y, y, weight, None, ALU.mult)
                return last

            def keep_turned(m, gain):
                for b in range(KD // 2):
                    dve.wait_ge(turned_high, KD // 2 * m + b + 1)
                    if gain is None:
                        V.tensor_tensor(xTl[:, 2 * b:2 * b + 2, :].rearrange("p k s -> p (k s)"), wk[:, b, :],
                                        xTh[:, 2 * b:2 * b + 2, :].rearrange("p k s -> p (k s)").bitcast(F32),
                                        ALU.subtract).then_inc(turned_kept, 1)
                    else:
                        for k in (2 * b, 2 * b + 1):
                            ins = V.scalar_tensor_tensor(xTl[:, k, :], wk[:, b, (k % 2) * S:(k % 2 + 1) * S],
                                                         gain[:, k:k + 1], xTh[:, k, :].bitcast(F32),
                                                         ALU.mult, ALU.subtract)
                        ins.then_inc(turned_kept, 1)

            def rms_scale(squares, weight=1.0):
                dve.wait_ge(squares_ready, squares)
                chain.link(V.tensor_scalar(stat[:, 2:4], stat[:, 0:2], 1.0 / D, EPS, ALU.mult, ALU.add))
                rsqrt(stat[:, 2:4], stat[:, 6:8], stat[:, 8:10], weight).then_inc(scale_ready, 1)

            def rms_in(scales, m, U, gain):
                rms_scale(T * (scales + 1))
                dve.wait_ge(scale_ready, scales + 1)
                V.tensor_scalar(xn[:, 0, :], x[:, 0, :], stat[:, 8:9], None, ALU.mult).then_inc(rows_v, 1)
                split_to(U + RING)
                keep_turned(m, gain)

            def rms_out(scales, nv, weight):
                rms_scale(T * (scales + 1), weight)
                dve.wait_ge(scale_ready, scales + 1)
                dve.wait_ge(vec_loaded[nv % 3], 16 * (nv // 3 + 1))
                for t in range(T):
                    chain.link(V.scalar_tensor_tensor(xn[:, t, :], acc[:, t, :], stat[:, 8 + t:9 + t],
                                                      vec[:, nv % 3, :], ALU.mult, ALU.mult))
                    V.tensor_tensor(x[:, t, :], x[:, t, :], xn[:, t, :], ALU.add).then_inc(x_ready, 1)

            def hidden_step(H, r, i, body, bank, buffer, gate, up, down):
                h = H + r
                if up is not None:
                    split(gate + 3, i)
                    dve.wait_ge(unit_done, up + 1 + LOOP_UNITS * i)
                dve.wait_ge(act_ready, h + 1 + body * i)
                e = hid[:, buffer, :]
                V.tensor_tensor(e, e, wk[:, bank, :], ALU.mult).then_inc(hidden_made, 1)
                split((up if up is not None else gate) + 3, i)
                dve.wait_ge(hidden_high, h + 1 + body * i)
                V.tensor_tensor(hTl[:, buffer].rearrange("p k s -> p (k s)"), e,
                                hTh[:, buffer].rearrange("p k s -> p (k s)").bitcast(F32),
                                ALU.subtract).then_inc(hidden_ready, 1)
                if down is not None:
                    split(down + 3, i)

            def ffn(U, H):
                def step(r, i):
                    gate, up, down = ffn_units(U, r)
                    hidden_step(H, r, i, FFN_BODY, 2 * (r % 2) + 1, r % 2, gate, up, down if r else None)
                split_to(U + RING)
                for r in range(FFN_FIRST):
                    step(r, 0)
                with dve.Fori(0, FFN_TRIPS) as i:
                    for r in range(FFN_FIRST, FFN_FIRST + FFN_BODY):
                        step(r, i)
                next_unit[0] = U + 3 * FG + 2

            def mlp(U, H):
                def step(r, i):
                    up, down = mlp_units(U, r)
                    hidden_step(H, r, i, MLP_BODY, r % 3, r % 3, up, None, down if r else None)
                split_to(U + RING)
                for r in range(MLP_FIRST):
                    step(r, 0)
                with dve.Fori(0, MLP_TRIPS) as i:
                    for r in range(MLP_FIRST, MLP_FIRST + MLP_BODY):
                        step(r, i)
                next_unit[0] = U + 2 * MG + 2

            def sb_stage(U):
                for j in range(12):
                    if j == 3:
                        dve.wait_ge(unit_done, U + 4)
                        for t in range(T):
                            ins = V.tensor_copy(sb_v[:, t, :], acc[:, t, :])
                        ins.then_inc(sbs["v_kept"], 1)
                    if 4 <= j < 8:
                        dve.wait_ge(unit_done, U + j + 1)
                        V.tensor_scalar(sb_q[:, 2 * (j - 4):2 * (j - 3), :].rearrange("p j s -> p (j s)"), wk[:, j - 4, :],
                                        HD ** -0.5, None, ALU.mult).then_inc(sbs["q_kept"], 1)
                    split_to(U + RING + j + 1)

                def absolute(h):
                    dve.wait_ge(sbs["z_ready"], h + 1)
                    if h >= 3:
                        dve.wait_ge(sbs["logits_ready"], h - 2)
                    V.tensor_scalar(hid[:, h % 3, 0:QB].bitcast(I32), wk[:, h % 4, 0:QB].bitcast(I32), 0x7fffffff, None,
                                    ALU.bitwise_and).then_inc(sbs["abs_ready"], 1)

                def softplus(h):
                    dve.wait_ge(sbs["log_ready"], h + 1)
                    e = hid[:, h % 3, 0:QB]
                    chain.link(V.scalar_tensor_tensor(e, wk[:, h % 4, 0:QB], 0.0, e, ALU.max, ALU.add))
                    V.tensor_tensor(diagonal(e), diagonal(e), later[:, :].unsqueeze(1).broadcast_to([P, 2, P]),
                                    ALU.mult).then_inc(sbs["softplus_ready"], 1)

                def pair_low(j):
                    dve.wait_ge(sbs["out_high"], j + 1)
                    V.tensor_tensor(xTl[:, j, :], acc[:, j % 2, 0:S], xTh[:, j, :].bitcast(F32),
                                    ALU.subtract).then_inc(sbs["out_kept"], 1)

                dve.wait_ge(masks_ready, 2)
                absolute(0)
                absolute(1)
                for h in range(HEADS):
                    if h + 2 < HEADS:
                        absolute(h + 2)
                    softplus(h)
                    if h % 2 == 0 and h:
                        pair_low(h // 2 - 1)
                pair_low(PAIRS - 1)
                split_to(U + 16)

            def keep_fills(sm, fills, first, dst, width, shift=0):
                for f in fills:
                    if f % 2:
                        dve.wait_ge(sm["fill_ready"], f - first + 1)
                        j = f - fills[0]
                        V.tensor_copy(dst[0:width, 2 * j:2 * j + 2, :], wk[0:width, (f + shift) % 4, :].rearrange(
                            "p (e s) -> p e s", e=2)).then_inc(sm["fill_v"], 1)

            def attention(sm, scale, bias, sink, mixed_before):
                def maxima(h):
                    dve.wait_ge(sm["scores_ready"], h + 1)
                    if h >= 3:
                        dve.wait_ge(sm["probs_turned"], h - 2)
                    e = hid[:, h % 3, 0:QB]
                    chain.link(V.scalar_tensor_tensor(e, wk[:, h % 2, 0:QB], scale, bias[:, :], ALU.mult, ALU.add))
                    both = att_stat[:, NMAX, 2 * h:2 * h + 2]
                    ins = V.tensor_reduce(both[:, 0:1], e[:, 0:P], AX.X, ALU.max, negate=True)
                    if sink:
                        chain.count(ins)
                    ins = V.tensor_reduce(both[:, 1:2], e[:, P:QB], AX.X, ALU.max, negate=True)
                    if sink:
                        chain.link(ins)
                        ins = V.tensor_scalar(both, both, minus_sinks[:, h:h + 1], None, ALU.min)
                    ins.then_inc(sm["max_ready"], 1)

                def sink_terms(c):
                    n = slice(HEADS * c, HEADS * c + HEADS)
                    dve.wait_ge(sm["max_ready"], 8 * c + 8)
                    V.tensor_tensor(att_stat[:, SINKX, n].rearrange("p (h t) -> p h t", t=T),
                                    att_stat[:, NMAX, n].rearrange("p (h t) -> p h t", t=T),
                                    sinks[:, 8 * c:8 * c + 8].unsqueeze(2).broadcast_to([P, 8, T]),
                                    ALU.add).then_inc(sm["sum_read"], 1)

                def outputs(c):
                    dve.wait_ge(sm["out_ready"], 8 * c + 8)
                    n = slice(HEADS * c, HEADS * c + HEADS)
                    if sink:
                        dve.wait_ge(sm["sink_exp"], c + 1)
                        chain.link(V.tensor_tensor(att_stat[:, SUMS, n], att_stat[:, SUMS, n], att_stat[:, SMALL, n], ALU.add))
                    chain.link(V.reciprocal(att_stat[:, RECIP, n], att_stat[:, SUMS, n]))
                    r = att_stat[:, RECIP, n].rearrange("p (h t) -> p h t", t=T)
                    for t in range(T):
                        ins = V.tensor_tensor(xn[:, t, c * BANK:(c + 1) * BANK].rearrange("p (h w) -> p h w", w=HD),
                                              acc[:, t, c * BANK:(c + 1) * BANK].rearrange("p (h w) -> p h w", w=HD),
                                              r[:, :, t:t + 1].broadcast_to([P, 8, HD]), ALU.mult)
                        if c:
                            ins.then_inc(mixed, 1)

                for h in range(HEADS):
                    maxima(h)
                    if h in (7, 15) and sink:
                        sink_terms(h // 8)
                    if h == 11:
                        outputs(0)
                outputs(1)

            def mla_stage(U, outs):
                split_to(U + 4)
                dve.wait_ge(mla_s["squares"], 4)
                chain.count(V.tensor_scalar(stat[:, 20:22], stat[:, 16:18], 1.0 / Q_LORA, EPS, ALU.mult, ALU.add))
                chain.link(V.tensor_scalar(stat[:, 22:24], stat[:, 18:20], 1.0 / KV_LORA, EPS, ALU.mult, ALU.add))
                chain.link(rsqrt(stat[:, 20:24], stat[:, 24:28], stat[:, 28:32]))
                chain.count(V.memset(xn[:, :, 3 * P:3 * P + NOPE], 0.0))
                for t in range(T):
                    chain.count(V.tensor_scalar(xn[:, t, 0:Q_LORA], acc[:, t, 0:Q_LORA], stat[:, 28 + t:29 + t], None, ALU.mult))
                    chain.count(V.tensor_scalar(xn[:, t, Q_LORA:3 * P], acc[:, t, Q_LORA:3 * P], stat[:, 30 + t:31 + t],
                                                None, ALU.mult))
                k = xn[:, :, 3 * P + NOPE:3 * P + MLA_W]
                chain.link(V.tensor_copy(k, acc[:, :, 3 * P:MLA_IN]))
                dve.wait_ge(trig_ready, 1)
                rope(V, chain, k.unsqueeze(2), sin1, cos1, ROPE // 2).then_inc(mla_s["c_rows"], 1)
                split_to(U + 5)
                dve.wait_ge(mla_s["c_high"], 1)
                for k, at in ((0, 0), (1, S)):
                    V.scalar_tensor_tensor(xTl[:, k, :], wk[:, 0, at:at + S], gain_cols[:, 96 + k:97 + k],
                                           xTh[:, k, :].bitcast(F32), ALU.mult, ALU.subtract).then_inc(mla_s["c_kept"], 1)
                dve.wait_ge(mla_s["c_high"], 2)
                V.scalar_tensor_tensor(xTl[:, 2, :], wk[:, 1, 0:S], gain_cols[:, 98:99],
                                       xTh[:, 2, :].bitcast(F32), ALU.mult, ALU.subtract).then_inc(mla_s["c_kept"], 1)
                dve.wait_ge(mla_s["c_turned"], 4)
                V.tensor_copy(mla_kT[NOPE:MLA_W, 0, :], wk[NOPE:MLA_W, 2, 0:S]).then_inc(mla_s["c_kept"], 1)
                dve.wait_ge(unit_done, U + 4)
                V.tensor_copy(work[:, 1536 + D:1536 + D + BANK], wk[:, 1, :]).then_inc(mla_s["fill_v"], 1)
                for t in range(T):
                    ins = V.tensor_copy(work[:, 1536 * t:1536 * t + D], acc[:, t, :])
                ins.then_inc(mla_s["rows_kept_v"], 1)
                split_to(U + 7)
                keep_fills(mla_s, range(2, 10), 2, mla_kT, NOPE)
                dve.wait_ge(unit_done, U + 5)
                for t in range(T):
                    ins = V.tensor_copy(mla_v[:, t, :], acc[:, t, :])
                ins.then_inc(mla_s["v_kept"], 1)
                split_to(U + 8)
                keep_fills(mla_s, range(10, 18), 2, mla_qT, MLA_W)
                dve.wait_ge(bias_ready, 3)
                attention(mla_s, MLA_W ** -0.5, causal, False, outs)

            def mlstm_stage(U):
                split_to(U + 8)
                dve.wait_ge(ml["bias_loaded"], 32)
                dve.wait_ge(unit_done, U + 5)
                V.tensor_tensor(ml_pre, wk[:, 0, 0:16].rearrange("p (t n) -> p t n", t=T),
                                gate_bias[:, :].unsqueeze(1).broadcast_to([P, T, 8]), ALU.add).then_inc(ml["biased"], 1)
                dve.wait_ge(ml["tanh"], 1)
                chain.link(V.tensor_scalar(ml_small[:, 0:16], ml_small[:, 0:16], GATE_CAP, None, ALU.mult))
                forget = ml_pre[:, :, M_HEADS:8]
                V.tensor_scalar(ml_log.bitcast(I32), forget.bitcast(I32), 0x7fffffff, None,
                                ALU.bitwise_and).then_inc(ml["abs"], 1)
                dve.wait_ge(ml["log"], 1)
                V.scalar_tensor_tensor(forget, forget, 0.0, ml_log, ALU.min, ALU.subtract).then_inc(ml["gates_ready"], 1)
                chain.link(V.memset(ML_ONES, 1.0))
                split_to(U + 10)
                dve.wait_ge(ml["gates_turned"], 1)
                chain.link(V.tensor_tensor_scan(ML_F, ML_ONES, wk[0:M_HEADS, 1, S:2 * S], 0.0, ALU.mult, ALU.add))
                chain.link(V.tensor_tensor(ML_G, wk[0:M_HEADS, 1, 0:S], ML_F, ALU.subtract))
                chain.link(V.tensor_tensor_scan(ML_M, ML_G, ML_G, 0.0, ALU.max, ALU.max))
                V.tensor_tensor(ML_FLOOR, ML_F, ML_M, ALU.add).then_inc(ml["m_ready"], 1)
                split_to(U + 12)
                dve.wait_ge(ml["cols_turned"], 1)
                V.tensor_copy(ml_small[:, 32:48], wk[:, 2, 0:16]).then_inc(ml["cols_kept"], 1)
                dve.wait_ge(ml["cols_kept"], 1)
                for h in range(M_HEADS):
                    dve.wait_ge(ml["spread"], h // 2 + 1)
                    minus_m = wk[:, (3, 0)[h // 2], (h % 2) * S:(h % 2 + 1) * S]
                    e = ml_decay[:, h, :]
                    V.scalar_tensor_tensor(e[:, 0:S], minus_m, ml_cols[:, 0, 0, h:h + 1], ml_bound[:, 0:S], ALU.add, ALU.min)
                    V.scalar_tensor_tensor(e[:, S:QB], minus_m[:, P:S], ml_cols[:, 0, 1, h:h + 1], ml_bound[:, S:QB],
                                           ALU.add, ALU.min).then_inc(ml["bounded"], 1)
                split_to(U + 13)
                dve.wait_ge(unit_done, U + 9)
                for t in range(T):
                    ins = V.tensor_copy(ml_v[:, t, :], acc[:, t, :])
                ins.then_inc(ml["v_kept"], 1)
                split_to(U + 15)
                for j in range(2):
                    dve.wait_ge(unit_done, U + 12 + j)
                    V.tensor_copy(ml_k[:, 2 * j:2 * j + 2, :].rearrange("p h s -> p (h s)"),
                                  wk[:, (3, 0)[j], :]).then_inc(ml["k_kept"], 1)
                    split_to(U + 16)
                for h in range(M_HEADS):
                    dve.wait_ge(ml["decay_ready"], h + 1)
                    dve.wait_ge(ml["scores_ready"], h + 1)
                    V.tensor_tensor(ml_scores[:, h, :], wk[:, h, 0:QB], ml_decay[:, h, :],
                                    ALU.mult).then_inc(ml["weights_ready"], 1)
                for h in range(M_HEADS):
                    if h % 2 == 0:
                        dve.wait_ge(ml["out_ready"], h + 2)
                    for t in range(T):
                        j = T * h + t
                        chain.count(V.bn_stats(ml_small[:, 48 + 6 * j:54 + 6 * j], acc[:, t, h * M_DV:(h + 1) * M_DV]))
                den = ml_inv.rearrange("p (h t) -> p h t", t=T)
                chain.link(V.tensor_scalar(den.bitcast(I32), wk[:, :, QB:QB + T].bitcast(I32), 0x7fffffff, None,
                                           ALU.bitwise_and))
                for j in range(T * M_HEADS):
                    chain.count(V.bn_aggr(ml_small[:, 96 + 2 * j:98 + 2 * j], ml_small[:, 48 + 6 * j:54 + 6 * j]))
                chain.link(V.tensor_tensor(den, den, ml_cols[:, 1].rearrange("p t h -> p h t"), ALU.max))
                chain.link(V.reciprocal(ml_inv, ml_inv))
                var = ml_var.rearrange("p (h t) -> p h t", t=T)
                chain.link(V.tensor_tensor(var, ml_moments[:, :, :, 1], den, ALU.mult))
                chain.link(V.tensor_tensor(ml_var, ml_var, ml_inv, ALU.mult))
                chain.link(V.tensor_scalar(ml_var, ml_var, LN_EPS, None, ALU.add))
                chain.link(rsqrt(ml_var, ml_half, ml_rs))
                chain.link(V.tensor_tensor(ml_scale, ml_rs, ml_inv, ALU.mult))
                for t in range(T):
                    for h in range(M_HEADS):
                        j = T * h + t
                        c = slice(h * M_DV, (h + 1) * M_DV)
                        ins = V.tensor_scalar(xn[:, t, c], acc[:, t, c], ml_moments[:, h, t, 0:1], ml_scale[:, j:j + 1],
                                              ALU.subtract, ALU.mult)
                        if h < M_HEADS - 1:
                            chain.count(ins)
                    chain.link(ins)
                    dve.wait_ge(ml["gated"], t + 1)
                    V.tensor_tensor(xn[:, t, :], xn[:, t, :], ml_gate[:, t, :], ALU.mult).then_inc(mixed, 1)

            def swa_stage(U, outs, nv):
                split_to(U + 4)
                dve.wait_ge(unit_done, U + 2)
                dve.wait_ge(vec_loaded[nv % 3], 16 * (nv // 3 + 1))
                for t in range(T):
                    ins = V.tensor_tensor(swa_kv[:, t, :], wk[:, t, :], vec[:, nv % 3, 0:BANK], ALU.add)
                ins.then_inc(swa_s["rows_kept_v"], 1)
                split_to(U + 8)
                dve.wait_ge(unit_done, U + 6)
                nv += 1
                dve.wait_ge(vec_loaded[nv % 3], 16 * (nv // 3 + 1))
                for t in range(T):
                    ins = V.tensor_tensor(work[:, D * t:D * t + D], acc[:, t, :], vec[:, nv % 3, :], ALU.add)
                ins.then_inc(swa_s["rows_kept_v"], 1)
                split_to(U + 9)
                keep_fills(swa_s, range(0, 2), 0, swa_kT, HD, 2)
                keep_fills(swa_s, range(2, 10), 0, swa_qT, HD, 2)
                dve.wait_ge(bias_ready, 3)
                dve.wait_ge(sinks_loaded, 16)
                chain.link(V.tensor_scalar(minus_sinks[:, :], sinks[:, :], -1.0, None, ALU.mult))
                attention(swa_s, HD ** -0.5, window, True, outs)

            def moments(rows, at, n):
                for j in range(n):
                    for c in range(2):
                        b = 40 + 12 * j + 6 * c
                        ins = V.bn_stats(stat[:, b:b + 6], rows(j, c))
                        if (j, c) != (n - 1, 1):
                            chain.count(ins)
                chain.link(ins)
                for j in range(n):
                    ins = V.bn_aggr(stat[:, at + 2 * j:at + 2 * j + 2], stat[:, 40 + 12 * j:52 + 12 * j])
                    if j < n - 1:
                        chain.count(ins)
                chain.link(ins)

            def layer_norm(end, nv, bias):
                dve.wait_ge(unit_done, end)
                for t in range(T):
                    chain.link(V.scalar_tensor_tensor(x[:, t, :], x[:, t, :], ALPHA, acc[:, t, :], ALU.mult, ALU.add))
                    if bias is not None:
                        dve.wait_ge(vec_loaded[bias % 3], 16 * (bias // 3 + 1))
                        chain.link(V.tensor_tensor(x[:, t, :], x[:, t, :], vec[:, bias % 3, :], ALU.add))
                moments(lambda j, c: x[:, j, c * BANK:(c + 1) * BANK], 10, T)
                v = stat[:, 10:14].rearrange("p (t c) -> p t c", c=2)
                chain.link(V.tensor_scalar(stat[:, 2:4], v[:, :, 1], LN_EPS, None, ALU.add))
                chain.link(rsqrt(stat[:, 2:4], stat[:, 6:8], stat[:, 8:10]))
                for n in (nv, nv + 1):
                    dve.wait_ge(vec_loaded[n % 3], 16 * (n // 3 + 1))
                for t in range(T):
                    chain.link(V.tensor_scalar(x[:, t, :], x[:, t, :], v[:, t, 0:1], stat[:, 8 + t:9 + t],
                                               ALU.subtract, ALU.mult))
                    chain.link(V.tensor_tensor(x[:, t, :], x[:, t, :], vec[:, nv % 3, :], ALU.mult))
                    V.tensor_tensor(x[:, t, :], x[:, t, :], vec[:, (nv + 1) % 3, :], ALU.add).then_inc(x_ready, 1)

            def ple_stage(U, n, m):
                dve.wait_ge(ple_s["high"], n + 1)
                V.tensor_tensor(hTl[:, 0].rearrange("p k s -> p (k s)"), wk[:, 0, :],
                                hTh[:, 0].rearrange("p k s -> p (k s)").bitcast(F32), ALU.subtract).then_inc(ple_s["kept"], 1)
                split_to(U + RING)
                keep_turned(m, None)
                split_to(U + 7)

            def ple_out(U, n, nv):
                dve.wait_ge(unit_done, U + 5)
                dve.wait_ge(vec_loaded[nv % 3], 16 * (nv // 3 + 1))
                for t in range(T):
                    V.tensor_tensor(xn[:, t, :], acc[:, t, :], vec[:, nv % 3, :], ALU.add).then_inc(ple_s["biased"], 1)
                for t in range(T):
                    dve.wait_ge(ple_s["gate"], T * n + t + 1)
                    chain.link(V.tensor_tensor(xn[:, t, :], xn[:, t, :],
                                               wk[:, 2 * t:2 * t + 2, :].rearrange("p c n -> p (c n)"), ALU.mult))
                for t in range(T):
                    V.tensor_tensor(x[:, t, :], x[:, t, :], xn[:, t, :], ALU.add).then_inc(x_ready, 1)

            def positions():
                dve.wait_ge(pos_loaded, 32)
                V.tensor_copy(pos_rows[:, :], pos_i[:, :]).then_inc(pos_made, 1)
                dve.wait_ge(pos_turned, 1)
                chain.link(V.tensor_copy(pos[:, :], wk[:, 2, 0:4]))
                dve.wait_ge(freq_ready, 24)
                for col, t, f, n in ((0, 0, 0, 16), (16, 1, 0, 16), (32, 2, 16, 8), (40, 3, 16, 8)):
                    chain.link(V.tensor_scalar(angle[:, col:col + n], inv_freq[:, f:f + n], pos[:, t:t + 1], None, ALU.mult))
                chain.link(V.tensor_copy(angle[:, 48:96], angle[:, 0:48]))
                chain.link(V.tensor_scalar(turns[:, 0:48], angle[:, 0:48], INV_TURN, None, ALU.mult))
                chain.link(V.tensor_scalar(turns[:, 48:96], angle[:, 48:96], INV_TURN, 0.25, ALU.mult, ALU.add))
                chain.link(V.tensor_copy(turns_i[:, :], turns[:, :]))
                chain.link(V.tensor_copy(turns[:, :], turns_i[:, :]))
                for part in TURN_PARTS:
                    chain.link(V.scalar_tensor_tensor(angle[:, :], turns[:, :], -part, angle[:, :], ALU.mult, ALU.add))
                chain.link(V.tensor_scalar(angle[:, 48:96], angle[:, 48:96], float(np.pi / 2), None, ALU.add))
                V.tensor_scalar(angle[:, :], angle[:, :], SIN_MAX, -SIN_MAX, ALU.min, ALU.max).then_inc(angles_ready, 1)

            dve.wait_ge(gains_turned, 1)
            V.tensor_copy(gain_cols[:, :], wk[:, 3, 0:NG]).then_inc(gains_kept, 1)
            positions()
            outs = 0
            m = hidden = scales = nv = 0
            for s, (name, U, n) in enumerate(plan):
                if name in ("ffn", "sb", "mla"):
                    col = {"ffn": (6 * (n // 2) + 4 * (n % 2)), "sb": 2, "mla": 8}[name] * KD
                    rms_in(scales, m, U, gain_cols[:, col:col + KD])
                    m, scales = m + 1, scales + 1
                if name == "ffn":
                    ffn(U, hidden)
                    hidden += FG
                if name == "sb":
                    sb_stage(U)
                if name == "mla":
                    mla_stage(U, outs)
                if name in ("mlstm", "mlp", "swa"):
                    split_to(U + RING)
                    keep_turned(m, None)
                    m += 1
                if name == "mlp":
                    mlp(U, hidden)
                    hidden += MG
                if name == "mlstm":
                    mlstm_stage(U)
                if name == "swa":
                    swa_stage(U, outs, nv)
                if name == "ple":
                    ple_stage(U, n, m)
                    m += 1
                if name in ("mla", "mlstm", "swa"):
                    keep_turned(m, None)
                    m, outs = m + 1, outs + 1
                    split_to(U + STAGE_UNITS[name] + 2)
                if name in ("ffn", "sb", "mla"):
                    rms_out(scales, nv, 0.5 if name == "ffn" else 1.0)
                    scales += 1
                if name in ("mlstm", "mlp", "swa"):
                    layer_norm(U + STAGE_UNITS[name], nv + VECTORS_USED[name] - 2, nv + 2 if name == "swa" else None)
                if name == "ple":
                    ple_out(U, n, nv)
                nv += VECTORS_USED[name]


def kernel(**inputs):
    import numpy as _np
    import concourse.bacc as _bacc
    from concourse.bass_utils import run_bass_kernel_spmd as _run

    nc = _bacc.Bacc("TRN2", target_bir_lowering=False, num_devices=1)
    arrays, aps = {}, {}
    for name, value in inputs.items():
        v = _np.ascontiguousarray(value)
        arrays[name + "_dram"] = v
        aps[name] = nc.dram_tensor(name + "_dram", v.shape, mybir.dt.from_np(v.dtype), kind="ExternalInput").ap()
    out = nc.dram_tensor("out_dram", (1, S, D), F32, kind="ExternalOutput").ap()
    build(nc, aps, out)
    return _run(nc, [arrays], core_ids=[0]).results[0]["out_dram"]
```

```python
from contextlib import ExitStack

import numpy as np

import concourse.bass as bass
from concourse import mybir

F32 = mybir.dt.float32
F32R = mybir.dt.float32r
I32 = mybir.dt.int32
ALU = mybir.AluOpType
ACT = mybir.ActivationFunctionType
AX = mybir.AxisListType

P = 128
S = 256
T = S // P
D = 1024
KD = D // P
BANK = 512
RING = 3
UNIT = 2048
GW = 256
FF = 2816
FG = FF // GW
FF2 = 4096
MG = FF2 // GW
EPS = 1e-6
LN_EPS = 1e-5
LOOP_UNITS = 6
FFN_FIRST, FFN_BODY, FFN_TRIPS = 3, 2, 3
FFN_LAST = FFN_FIRST + FFN_BODY * FFN_TRIPS
MLP_FIRST, MLP_BODY, MLP_TRIPS = 4, 3, 3
MLP_LAST = MLP_FIRST + MLP_BODY * MLP_TRIPS
HEADS = 16
HD = 64
PAIRS = HEADS // 2
QB = 3 * P
NG = 12 * KD + 3
Q_LORA, KV_LORA, ROPE, NOPE = 256, 128, 32, 64
MLA_IN = Q_LORA + KV_LORA + ROPE
MLA_W = NOPE + ROPE
MLA_COPIES = (1, 4), (4, 16)
KV_HEADS = 4
ROPE2 = 16
M_HEADS = 4
M_DK = 128
M_DV = 256
GATE_CAP = 15.0
PLE = 256
ALPHA = 4 ** 0.25
MASKED = -1e30
INV_TURN = float(1 / (2 * np.pi))
TURN_PARTS = (6.28125, 2029 / 2 ** 20, float(2 * np.pi - 6.28125 - 2029 / 2 ** 20))
SIN_MAX = 3.1415925

STAGE_UNITS = {"ffn": 3 * FG, "sb": 16, "mla": 9, "mlstm": 17, "swa": 10, "mlp": 2 * MG, "ple": 5}
VECTORS_USED = {"ffn": 1, "sb": 1, "mla": 1, "mlstm": 3, "swa": 5, "mlp": 2, "ple": 1}
STAGES = ["ffn", "sb", "ffn", "ffn", "mla", "ffn", "mlstm", "mlp", "ple", "swa", "mlp", "ple"]


class Chain:

    def __init__(self, eng, sem):
        self.eng, self.sem, self.n = eng, sem, 0

    def link(self, ins):
        self.n += 1
        ins.then_inc(self.sem, 1)
        self.eng.wait_ge(self.sem, self.n)

    def count(self, ins):
        self.n += 1
        ins.then_inc(self.sem, 1)


def inverse_frequencies(theta, width):
    return (np.float32(theta) ** (-(np.arange(0, width, 2, dtype=np.float32) / np.float32(width)))).astype(np.float32)


def build(nc, a, out):
    ctx = ExitStack()
    with ctx:
        def sb(name, shape, dt=F32):
            return ctx.enter_context(nc.sbuf_tensor(name, shape, dt))

        def sem(name):
            return ctx.enter_context(nc.semaphore(name))

        x = sb("x_rows", [P, T, D])
        xn = sb("scratch_rows", [P, T, D])
        xTh = sb("turned_high", [P, KD, S], F32R)
        xTl = sb("turned_low", [P, KD, S], F32R)
        raw = sb("weights_raw", [P, RING, UNIT])
        whi = sb("weights_high", [P, RING, UNIT], F32R)
        wlo = sb("weights_low", [P, RING, UNIT], F32R)
        hTh = sb("hidden_high", [P, 3, 2, S], F32R)
        hTl = sb("hidden_low", [P, 3, 2, S], F32R)
        hid = sb("hidden", [P, 3, BANK])
        vec = sb("row_vectors", [P, 3, D])
        gain_rows = sb("gain_rows", [NG, P])
        gain_cols = sb("gain_columns", [P, NG])
        square_out = sb("square_out", [P, T, D])
        ident = sb("identity", [P, P])
        scales = sb("rms_scales", [P, T, P])
        eps = sb("eps", [P, 3])
        stat = sb("stat", [P, 64])
        work = sb("work", [P, 13312])
        probs_T = sb("probs_turned", [P, 2, QB])
        neg_tri = sb("minus_lower", [P, P])
        neg_ones = sb("minus_ones", [P, P])
        later = sb("later_mask", [P, P])
        causal = sb("causal_bias", [P, QB])
        window = sb("window_bias", [P, QB])
        pos_i = sb("positions_int", [4, P], I32)
        pos_rows = sb("positions_rows", [4, P])
        pos = sb("positions", [P, 4])
        inv_freq = sb("inverse_frequencies", [P, 24])
        angle = sb("angle", [P, 96])
        turns = sb("whole_turns", [P, 96])
        turns_i = sb("whole_turns_int", [P, 96], I32)
        trig = sb("sines_cosines", [P, 96])
        att_stat = sb("attention_stat", [P, 5, 2 * HEADS])
        sinks = sb("sinks", [P, HEADS])
        minus_sinks = sb("minus_sinks", [P, HEADS])
        gate_bias = sb("gate_bias", [P, 2 * M_HEADS])

        acc = ctx.enter_context(nc.psum_tensor("acc", [P, T, D], F32))
        wk = ctx.enter_context(nc.psum_tensor("wk", [P, 4, BANK], F32))

        landed = [sem(f"unit_landed_{s}") for s in range(RING)]
        high_ready = sem("unit_high_ready")
        unit_ready = sem("unit_ready")
        unit_done = sem("unit_done")
        x_loaded = [sem(f"x_loaded_{t}") for t in range(T)]
        result = sem("result_ready")
        x_ready = sem("x_ready")
        gains_loaded = sem("gains_loaded")
        gains_turned = sem("gains_turned")
        gains_kept = sem("gains_kept")
        vec_loaded = [sem(f"vec_loaded_{s}") for s in range(3)]
        ident_ready = sem("ident_ready")
        std_ready = sem("root_mean_square_ready")
        eps_ready = sem("eps_ready")
        var_ready = sem("variance_ready")
        dev_ready = sem("deviation_ready")
        scales_ready = sem("rms_scales_ready")
        turned = sem("turned")
        turned_high = sem("turned_high_ready")
        turned_kept = sem("turned_kept")
        act_ready = sem("activation_ready")
        hidden_made = sem("hidden_made")
        hidden_high = sem("hidden_high_ready")
        hidden_ready = sem("hidden_ready")
        act_chain = sem("act_chain")
        dve_chain = sem("dve_chain")
        pool_chain = sem("pool_chain")
        pool_order = sem("pool_order")
        out_stored = sem("out_stored")
        pos_loaded = sem("positions_loaded")
        pos_made = sem("positions_float")
        pos_turned = sem("positions_turned")
        angles_ready = sem("angles_ready")
        trig_ready = sem("trig_ready")
        masks_ready = sem("masks_ready")
        freq_ready = sem("frequencies_ready")
        bias_ready = sem("bias_masks_ready")
        sinks_loaded = sem("sinks_loaded")
        mixed = sem("mixed")
        sbs = {n: sem("sb_" + n) for n in (
            "v_kept", "q_kept", "k_kept", "z_ready", "abs_ready", "log_ready", "softplus_ready", "logits_ready",
            "raw_ready", "weights_ready", "out_ready", "out_high", "out_kept")}

        block = ctx.enter_context(nc.Block())

        x_d = a["x"].rearrange("b (t p) d -> p (b t) d", p=P)
        out_d = out.rearrange("b (t p) d -> p (b t) d", p=P)

        def col_units(w):
            return w.rearrange("(k p) (g n) -> g p k n", p=P, n=GW)

        def row_units(w):
            return w.rearrange("(g k p) n -> g p k n", p=P, k=2)

        def quarter_units(w):
            return w.rearrange("(h k p) (c n) -> h c p k n", p=P, k=4, n=BANK)

        ffn_in = [[col_units(a["ffn_w_in"][l, f]) for f in range(2)] for l in range(2)]
        ffn_out = [[row_units(a["ffn_w_out"][l, f]) for f in range(2)] for l in range(2)]
        mlp_up = [col_units(a["mlp_w_up_2"][l]) for l in range(2)]
        mlp_down = [row_units(a["mlp_w_down_2"][l]) for l in range(2)]
        g = a["norm_g"]

        def row_vectors(name, n):
            return {"ffn": lambda: [g[n // 2, 1 + 4 * (n % 2)]], "sb": lambda: [g[0, 3]], "mla": lambda: [g[1, 3]],
                    "mlstm": lambda: [a["a_head_norm_g_2"][0], a["mix_ln_g_2"][0], a["mix_ln_b_2"][0]],
                    "swa": lambda: [a["kv_b_2"], a["b_b_q_2"][0], a["b_b_o_2"][0], a["mix_ln_g_2"][1], a["mix_ln_b_2"][1]],
                    "mlp": lambda: [a["mlp_ln_g_2"][n], a["mlp_ln_b_2"][n]], "ple": lambda: [a["ple_b_gate_2"][n]]}[name]()

        VECTORS = [(v, s, j) for s, name in enumerate(STAGES)
                   for j, v in enumerate(row_vectors(name, STAGES[:s].count(name)))]

        plan, at = [], 0
        for n, name in enumerate(STAGES):
            plan.append((name, at, STAGES[:n].count(name)))
            at += STAGE_UNITS[name]
        TOTAL = at

        def slot(tensor, u, k):
            return tensor[:, u % RING, :].rearrange("p (k n) -> p k n", k=k)

        def ffn_units(U, r):
            return U + max(3 * r - 1, 0), U + max(3 * r, 1), U + 3 * r + 1

        def mlp_units(U, r):
            return U + max(2 * r - 1, 0), U + 2 * r

        sb_q = work[:, 0:2048].rearrange("p (j s) -> p j s", s=S)
        sb_k = work[:, 2048:4096].rearrange("p (j s) -> p j s", s=S)
        sb_v = work[:, 4096:6144].rearrange("p (t d) -> p t d", t=T)
        sb_a = work[:, 6144:6144 + 3 * QB].rearrange("p (b n) -> p b n", b=3)

        mla_q = work[:, 0:3072].rearrange("p (t h w) -> p t h w", t=T, h=HEADS)
        mla_qT = work[0:MLA_W, 3072:7168].rearrange("p (h s) -> p h s", s=S)
        mla_kT = work[0:MLA_W, 7168:11264].rearrange("p (h s) -> p h s", s=S)
        mla_v = work[:, 11264:13312].rearrange("p (t d) -> p t d", t=T)
        swa_q = work[:, 0:2048].rearrange("p (t h w) -> p t h w", t=T, h=HEADS)
        swa_kv = work[:, 2048:3072].rearrange("p (t n) -> p t n", t=T)
        swa_qT = work[0:HD, 3072:7168].rearrange("p (h s) -> p h s", s=S)
        swa_kT = work[0:HD, 7168:8192].rearrange("p (h s) -> p h s", s=S)
        ml_q = work[:, 0:1024].rearrange("p (h s) -> p h s", s=S)
        ml_k = work[:, 1024:2048].rearrange("p (h s) -> p h s", s=S)
        ml_v = work[:, 2048:4096].rearrange("p (t d) -> p t d", t=T)
        ml_gate = work[:, 4096:6144].rearrange("p (t d) -> p t d", t=T)
        ml_scores = work[:, 6144:7680].rearrange("p (h n) -> p h n", n=QB)
        ml_decay = work[:, 7680:9216].rearrange("p (h n) -> p h n", n=QB)
        ml_bound = work[:, 9216:9600]
        ml_select = work[0:M_HEADS, 9600:10112]
        ML_ONES, ML_F, ML_G, ML_M, ML_FLOOR = [work[0:M_HEADS, c:c + S] for c in range(10112, 10112 + 5 * S, S)]
        ml_small = work[:, 11392:11392 + 152]
        ml_pre = ml_small[:, 0:16].rearrange("p (t n) -> p t n", t=T)
        ml_log = ml_small[:, 16:24].rearrange("p (t h) -> p t h", t=T)
        ml_cols = ml_small[:, 32:48].rearrange("p (c t h) -> p c t h", c=2, t=T)
        ml_moments = ml_small[:, 96:112].rearrange("p (h t c) -> p h t c", t=T, c=2)
        ml_inv, ml_var, ml_half, ml_rs, ml_scale = [
            ml_small[:, c:c + 8] for c in (112, 120, 128, 136, 144)]
        ml = {n: sem("mlstm_" + n) for n in (
            "consts", "bias_loaded", "o_kept", "gated", "biased", "tanh", "abs", "log", "gates_ready", "gates_turned",
            "m_ready", "floor_ready", "cols_turned", "spread", "cols_kept", "bounded", "decay_ready", "q_kept", "k_kept",
            "v_kept", "scores_ready", "weights_ready", "out_ready", "var_ready", "dev_ready")}
        sin1 = trig[:, 0:32].rearrange("p (t n) -> p t n", t=T)
        sin2 = trig[:, 32:48].rearrange("p (t n) -> p t n", t=T)
        cos1 = trig[:, 48:80].rearrange("p (t n) -> p t n", t=T)
        cos2 = trig[:, 80:96].rearrange("p (t n) -> p t n", t=T)
        NMAX, SUMS, RECIP, SINKX, SMALL = range(5)

        ATT = ("rows_kept_v", "roped", "roped_v", "k_copied", "fill_ready", "fill_a", "fill_v", "v_kept", "scores_ready",
               "max_ready", "probs_ready", "probs_turned", "probs_kept", "out_ready", "sum_read", "sink_exp",
               "squares", "c_rows", "c_turned", "c_high", "c_kept")
        mla_s = {n: sem("mla_" + n) for n in ATT}
        swa_s = {n: sem("swa_" + n) for n in ATT}
        p_loaded = sem("ple_rows_loaded")
        ple_s = {n: sem("ple_" + n) for n in ("turned", "high", "kept", "biased", "gate", "projected")}
        ple_rows = work[:, 12800:13312].rearrange("p (t n) -> p t n", t=T)

        def rope(E, order, rows, sin, cos, n, tiles=range(T)):
            heads = rows.shape[2]
            shape = [P, T, heads, n]
            size = T * heads * n
            prods = [square_out[:, :, :].rearrange("p t d -> p (t d)")[:, j * size:(j + 1) * size]
                     .rearrange("p (t h n) -> p t h n", t=T, h=heads) for j in range(4)]
            x1, x2 = rows[:, :, :, 0:n], rows[:, :, :, n:2 * n]
            for t in tiles:
                c = cos[:, t, :].unsqueeze(1).broadcast_to([P, heads, n])
                s_ = sin[:, t, :].unsqueeze(1).broadcast_to([P, heads, n])
                for dst, src, by in ((0, x1, c), (1, x2, s_), (2, x2, c), (3, x1, s_)):
                    last = E.tensor_tensor(prods[dst][:, t], src[:, t], by, ALU.mult)
                    if not (t == tiles[-1] and dst == 3):
                        order.count(last)
            order.link(last)
            for t in tiles:
                last = E.tensor_tensor(x1[:, t], prods[0][:, t], prods[1][:, t], ALU.subtract)
                order.count(last)
                last = E.tensor_tensor(x2[:, t], prods[2][:, t], prods[3][:, t], ALU.add)
                if t < tiles[-1]:
                    order.count(last)
            return last

        def diagonal(ap):
            return ap.rearrange("p (b n) -> p b n", n=P)[:, 0:3:2, :]

        @block.sync
        def _(sp):
            def load(u, i, src, k, n):
                if u >= RING:
                    sp.wait_ge(unit_ready, u - RING + 1 + LOOP_UNITS * i)
                sp.dma_start(slot(raw, u, k)[:, :, 0:n], src).then_inc(landed[u % RING], 16)

            def ffn(U, l, f):
                w_in, w_out = ffn_in[l][f], ffn_out[l][f]

                def step(r, i):
                    gate, up, down = ffn_units(U, r)
                    load(gate, i, w_in[r + FFN_BODY * i], 8, GW)
                    load(up, i, w_in[FG + r + FFN_BODY * i], 8, GW)
                    if r:
                        load(down, i, w_out[r - 1 + FFN_BODY * i], 2, D)

                for r in range(FFN_FIRST):
                    step(r, 0)
                with sp.Fori(0, FFN_TRIPS) as i:
                    for r in range(FFN_FIRST, FFN_FIRST + FFN_BODY):
                        step(r, i)
                for r in range(FFN_LAST, FG):
                    step(r, 0)
                load(U + 3 * FG - 1, 0, w_out[FG - 1], 2, D)

            def mlp(U, l):
                def step(r, i):
                    up, down = mlp_units(U, r)
                    load(up, i, mlp_up[l][r + MLP_BODY * i], 8, GW)
                    if r:
                        load(down, i, mlp_down[l][r - 1 + MLP_BODY * i], 2, D)

                for r in range(MLP_FIRST):
                    step(r, 0)
                with sp.Fori(0, MLP_TRIPS) as i:
                    for r in range(MLP_FIRST, MLP_FIRST + MLP_BODY):
                        step(r, i)
                for r in range(MLP_LAST, MG):
                    step(r, 0)
                load(U + 2 * MG - 1, 0, mlp_down[l][MG - 1], 2, D)

            def quarters(U, w, col=0, halves=2):
                w = quarter_units(w[:, col:col + halves * BANK])
                for c in range(halves):
                    for h in range(2):
                        load(U + 2 * c + h, 0, w[h, c], 4, BANK)

            def columns(U, w, col, n):
                w = col_units(w[:, col:col + n * GW])
                for j in range(n):
                    load(U + j, 0, w[j], 8, GW)

            for t in range(T):
                sp.dma_start(x[:, t, :], x_d[:, t, :]).then_inc(x_loaded[t], 16)
            sp.dma_start(gain_rows[0:12 * KD, :], g.rearrange("l n (k p) -> (l n k) p", p=P)).then_inc(gains_loaded, 16)
            sp.dma_start(gain_rows[12 * KD:12 * KD + 2, :],
                         a["mla_q_norm"].rearrange("l (k p) -> (l k) p", p=P)).then_inc(gains_loaded, 16)
            sp.dma_start(gain_rows[12 * KD + 2:NG, :], a["mla_kv_norm"]).then_inc(gains_loaded, 16)
            for t in range(2):
                sp.dma_start(pos_i[2 * t:2 * t + 2, :], a[("positions", "positions_2")[t]].rearrange(
                    "b (t p) -> (b t) p", p=P)).then_inc(pos_loaded, 16)
            for s, (name, U, n) in enumerate(plan):
                if name == "ffn":
                    ffn(U, n // 2, n % 2)
                if name == "sb":
                    w_in, w_out = a["sb_w_in"][0], a["sb_w_out"][0]
                    quarters(U, w_in, 2 * D)
                    columns(U + 4, w_in, 0, 8)
                    quarters(U + 12, w_out)
                if name == "mla":
                    w_in, w_uq, w_ukv = a["mla_w_in"][0], a["mla_w_uq"][0], a["mla_w_ukv"][0]
                    for h in range(2):
                        load(U + h, 0, w_in[h * BANK:(h + 1) * BANK, :].rearrange("(k p) n -> p k n", p=P), 4, MLA_IN)
                    w_uq = w_uq.rearrange("(k p) n -> p k n", p=P)
                    load(U + 2, 0, w_uq[:, :, 0:D], 2, D)
                    load(U + 3, 0, w_uq[:, :, D:D + BANK], 2, BANK)
                    load(U + 4, 0, w_ukv.rearrange("(k p) n -> p k n", p=P), 1, UNIT)
                    quarters(U + 5, a["mla_w_out"][0])
                if name == "mlstm":
                    w_in = a["a_w_in_2"][0]
                    quarters(U, w_in, 2 * D)
                    load(U + 4, 0, w_in[:, 3 * D:3 * D + 2 * M_HEADS].rearrange("(k p) n -> p k n", p=P), 8, 2 * M_HEADS)
                    quarters(U + 5, w_in, D)
                    columns(U + 9, w_in, 0, 4)
                    quarters(U + 13, a["a_w_out_2"][0])
                if name == "swa":
                    quarters(U, a["kv_w_2"], 0, 1)
                    quarters(U + 2, a["b_w_q_2"][0])
                    quarters(U + 6, a["b_w_o_2"][0])
                if name == "ple":
                    if s > 1:
                        sp.wait_ge(x_ready, T * (s - 1))
                    sp.dma_start(ple_rows, a["p_2"][n].rearrange("b (t p) n -> p (b t) n", p=P)).then_inc(p_loaded, 16)
                    quarters(U, a["ple_w_gate_2"][n])
                    load(U + 4, 0, row_units(a["ple_w_proj_2"][n])[0], 2, D)
                if name == "mlp":
                    mlp(U, n)
            for t in range(T):
                sp.wait_ge(x_ready, T * (len(STAGES) - 1) + t + 1)
                sp.dma_start(out_d[:, t, :], x[:, t, :]).then_inc(out_stored, 16)
            sp.wait_ge(out_stored, 16 * T)

        @block.gpsimd
        def _(pool):
            for j, value in enumerate((EPS, 4 * EPS, LN_EPS)):
                nc.gpsimd.memset(eps[:, j:j + 1], value).then_inc(eps_ready, 1)
            nc.gpsimd.memset(ident[:, :], 0.0).then_inc(pool_chain, 1)
            pool.wait_ge(pool_chain, 1)
            nc.gpsimd.affine_select(out=ident[:, :], in_=ident[:, :], compare_op=ALU.not_equal, fill=1.0,
                                    base=0, pattern=[[-1, P]], channel_multiplier=1).then_inc(ident_ready, 1)
            nc.gpsimd.memset(neg_tri[:, :], -1.0).then_inc(pool_chain, 1)
            nc.gpsimd.memset(neg_ones[:, :], -1.0).then_inc(pool_chain, 1)
            nc.gpsimd.memset(later[:, :], 1.0).then_inc(pool_chain, 1)
            pool.wait_ge(pool_chain, 4)
            nc.gpsimd.affine_select(out=neg_tri[:, :], in_=neg_tri[:, :], compare_op=ALU.is_ge, fill=0.0,
                                    base=0, pattern=[[-1, P]], channel_multiplier=1).then_inc(masks_ready, 1)
            nc.gpsimd.affine_select(out=later[:, :], in_=later[:, :], compare_op=ALU.is_gt, fill=0.0,
                                    base=0, pattern=[[1, P]], channel_multiplier=-1).then_inc(masks_ready, 1)

            for col, theta, width in ((0, 10000.0, ROPE), (16, 500000.0, ROPE2)):
                for j, f in enumerate(inverse_frequencies(theta, width)):
                    ins = nc.gpsimd.memset(inv_freq[:, col + j:col + j + 1], float(f))
                    ins.then_inc(freq_ready, 1)
            for bias in (causal, window):
                nc.gpsimd.memset(bias[:, :], 0.0).then_inc(pool_chain, 1)
            pool.wait_ge(pool_chain, 6)
            for bias in (causal, window):
                d = diagonal(bias[:, :])
                nc.gpsimd.affine_select(out=d, in_=d, compare_op=ALU.is_ge, fill=MASKED, base=0,
                                        pattern=[[0, 2], [-1, P]], channel_multiplier=1).then_inc(bias_ready, 1)
            nc.gpsimd.affine_select(out=window[:, P:S], in_=window[:, P:S], compare_op=ALU.is_gt, fill=MASKED, base=0,
                                    pattern=[[1, P]], channel_multiplier=-1).then_inc(bias_ready, 1)
            for j, b in enumerate(("a_b_igate_2", "a_b_fgate_2")):
                pool.dma_start(gate_bias[:, j * M_HEADS:(j + 1) * M_HEADS],
                               a[b][0].partition_broadcast(P)).then_inc(ml["bias_loaded"], 16)
            pool.dma_start(sinks[:, :], a["b_sinks_2"][0].partition_broadcast(P)).then_inc(sinks_loaded, 16)

            def mla_stage():
                pool.wait_ge(trig_ready, 1)
                pool.wait_ge(mla_s["fill_a"], 1)
                pool.wait_ge(mla_s["fill_v"], 1)
                pool.wait_ge(mla_s["rows_kept_v"], 1)
                rope(nc.gpsimd, order, mla_q[:, :, :, NOPE:MLA_W], sin1, cos1, ROPE // 2).then_inc(mla_s["roped"], 1)
                pool.wait_ge(mla_s["roped"], 1)
                pool.wait_ge(mla_s["c_kept"], 4)
                for h, end in MLA_COPIES:
                    nc.gpsimd.tensor_copy(mla_kT[NOPE:MLA_W, h:end, :],
                                          mla_kT[NOPE:MLA_W, 0:1, :].broadcast_to([ROPE, end - h, S]),
                                          ).then_inc(mla_s["k_copied"], 1)

            def mlstm_stage(s, nv):
                if s:
                    pool.wait_ge(x_ready, T * s)
                order.count(nc.gpsimd.memset(ml_bound, 0.0))
                order.link(nc.gpsimd.memset(ml_select, 0.0))
                d = diagonal(ml_bound)
                nc.gpsimd.affine_select(out=d, in_=d, compare_op=ALU.is_ge, fill=MASKED, base=0,
                                        pattern=[[0, 2], [1, P]], channel_multiplier=-1).then_inc(ml["consts"], 1)
                sel = ml_select.rearrange("p (h n) -> p h n", n=P)
                nc.gpsimd.affine_select(out=sel, in_=sel, compare_op=ALU.not_equal, fill=-1.0, base=0,
                                        pattern=[[-1, M_HEADS], [0, P]], channel_multiplier=1).then_inc(ml["consts"], 1)
                pool.wait_ge(vec_loaded[nv % 3], 16 * (nv // 3 + 1))
                for t in range(T):
                    pool.wait_ge(ml["o_kept"], t + 1)
                    nc.gpsimd.tensor_tensor(ml_gate[:, t, :], ml_gate[:, t, :], vec[:, nv % 3, :],
                                            ALU.mult).then_inc(ml["gated"], 1)

            def swa_stage():
                pool.wait_ge(trig_ready, 1)
                pool.wait_ge(swa_s["rows_kept_v"], 1)
                k = swa_kv[:, :, 0:KV_HEADS * HD].rearrange("p t (h w) -> p t h w", w=HD)
                rope(nc.gpsimd, order, k[:, :, :, 0:ROPE2], sin2, cos2, ROPE2 // 2).then_inc(swa_s["roped"], 1)
                pool.wait_ge(swa_s["roped"], 1)
                pool.wait_ge(swa_s["rows_kept_v"], 2)
                rope(nc.gpsimd, order, swa_q[:, :, :, 0:ROPE2], sin2, cos2, ROPE2 // 2, [0]).then_inc(swa_s["roped"], 1)

            def vectors(upto):
                while sent[0] < min(upto, len(VECTORS)):
                    n = sent[0]
                    if n >= 3:
                        _, s, j = VECTORS[n - 3]
                        if STAGES[s] == "swa" and j < 2:
                            pool.wait_ge(*((swa_s["rows_kept_v"], 1), (swa_s["roped_v"], 1))[j])
                        else:
                            pool.wait_ge(x_ready, T * (s + 1))
                    v = VECTORS[n][0]
                    pool.dma_start(vec[:, n % 3, 0:v.shape[0]], v.partition_broadcast(P)).then_inc(vec_loaded[n % 3], 16)
                    sent[0] += 1

            def sb_stage():
                for h in range(HEADS):
                    pool.wait_ge(sbs["raw_ready"], h + 1)
                    d = diagonal(sb_a[:, h % 3, :])
                    nc.gpsimd.affine_select(out=d, in_=d, compare_op=ALU.is_gt, fill=0.0, base=0,
                                            pattern=[[0, 2], [1, P]], channel_multiplier=-1,
                                            ).then_inc(sbs["weights_ready"], 1)

            order = Chain(pool, pool_order)
            sent, used = [0], 0
            for s, (name, U, n) in enumerate(plan):
                vectors(used + 3)
                if name == "sb":
                    sb_stage()
                if name == "mla":
                    mla_stage()
                if name == "mlstm":
                    mlstm_stage(s, used)
                if name == "swa":
                    swa_stage()
                    vectors(used + 5)
                used += VECTORS_USED[name]

        @block.tensor
        def _(pe):
            def wait_unit(u, i=0):
                pe.wait_ge(unit_ready, u + 1 + LOOP_UNITS * i)

            def product(dst, left, right, first, last):
                (lh, ll), (rh, rl) = left, right
                nc.tensor.matmul(dst, lh, rh, start=first, stop=False)
                nc.tensor.matmul(dst, lh, rl, start=False, stop=False)
                return nc.tensor.matmul(dst, ll, rh, start=False, stop=last)

            fresh = [None]

            def turn(m, src, ready, scaled=False):
                for t in range(T):
                    pe.wait_ge(*ready(t))
                    for k in range(KD):
                        dst = wk[:, k // 2, (k % 2) * S + t * P:(k % 2) * S + (t + 1) * P]
                        rows = src[:, t, k * P:(k + 1) * P]
                        if scaled:
                            mm = nc.tensor.matmul(dst, rows, scales[:, t, :], start=True, stop=True)
                        else:
                            mm = nc.tensor.transpose(dst, rows, ident[:, :])
                        if t == T - 1 and k % 2:
                            mm.then_inc(turned, 1)
                fresh[0] = m

            def wait_turned(k):
                if fresh[0] is not None and k % 2 == 0:
                    pe.wait_ge(turned_kept, KD // 2 * fresh[0] + k // 2 + 1)
                if k >= KD - 2:
                    fresh[0] = None

            def group_up(u, i, bank):
                wait_unit(u, i)
                wh, wl = slot(whi, u, 8), slot(wlo, u, 8)
                for h in range(2):
                    c = slice(h * P, (h + 1) * P)
                    for k in range(KD):
                        wait_turned(k)
                        mm = product(wk[:, bank, h * S:(h + 1) * S], (wh[:, k, c], wl[:, k, c]),
                                     (xTh[:, k, :], xTl[:, k, :]), k == 0, k == KD - 1)
                mm.then_inc(unit_done, 1)

            def down_tile(u, b, t, first, last):
                wh, wl = slot(whi, u, 2), slot(wlo, u, 2)
                r = slice(t * P, (t + 1) * P)
                for k in range(2):
                    for c in range(2):
                        n = slice(c * BANK, (c + 1) * BANK)
                        mm = product(acc[:, t, n], (hTh[:, b, k, r], hTl[:, b, k, r]),
                                     (wh[:, k, n], wl[:, k, n]), first and k == 0, last and k == 1)
                return mm

            def group_down(u, i, b, first):
                wait_unit(u, i)
                for t in range(T):
                    mm = down_tile(u, b, t, first, False)
                mm.then_inc(unit_done, 1)

            def last_down(u, hidden, buffers, r):
                for t in range(T):
                    for j in range(2):
                        if t == 0:
                            pe.wait_ge(hidden_ready, hidden + j)
                            wait_unit(u + j)
                        mm = down_tile(u + j, (r + j) % buffers, t, False, j == 1)
                        if t == T - 1:
                            mm.then_inc(unit_done, 1)
                    if t == 0:
                        mm.then_inc(result, 1)

            def row_tile(u, dst, k0, t, n):
                wh, wl = slot(whi, u, 4), slot(wlo, u, 4)
                r = slice(t * P, (t + 1) * P)
                for k in range(4):
                    if t == 0:
                        wait_turned(k0 + k)
                    mm = product(dst, (xTh[:, k0 + k, r], xTl[:, k0 + k, r]), (wh[:, k, 0:n], wl[:, k, 0:n]),
                                 k0 + k == 0, k0 + k == KD - 1)
                return mm

            def row_product(U, dst, halves=2, n=BANK, last=False):
                for c in range(halves):
                    u = U + 2 * c
                    if last and c == halves - 1:
                        for t in range(T):
                            for h in range(2):
                                if t == 0:
                                    wait_unit(u + h)
                                mm = row_tile(u + h, dst(t, c), 4 * h, t, n)
                                if t == T - 1:
                                    mm.then_inc(unit_done, 1)
                            if t == 0:
                                mm.then_inc(result, 1)
                    else:
                        for h in range(2):
                            wait_unit(u + h)
                            for t in range(T):
                                mm = row_tile(u + h, dst(t, c), 4 * h, t, n)
                            mm.then_inc(unit_done, 1)

            def ffn(U, H):
                def up(r, i):
                    gate, up, _ = ffn_units(U, r)
                    group_up(gate, i, 2 * (r % 2))
                    group_up(up, i, 2 * (r % 2) + 1)

                def down(r, i):
                    pe.wait_ge(hidden_ready, H + r + 1 + FFN_BODY * i)
                    group_down(ffn_units(U, r + 1)[2], i, r % 2, r == 0)

                up(0, 0)
                for r in range(1, FFN_FIRST):
                    up(r, 0)
                    down(r - 1, 0)
                with pe.Fori(0, FFN_TRIPS) as i:
                    for r in range(FFN_FIRST, FFN_FIRST + FFN_BODY):
                        up(r, i)
                        down(r - 1, i)
                for r in range(FFN_LAST, FG):
                    up(r, 0)
                    if r < FG - 1:
                        down(r - 1, 0)
                last_down(U + 3 * FG - 2, H + FG - 1, 2, FG - 2)

            def mlp(U, H):
                def up(r, i):
                    group_up(mlp_units(U, r)[0], i, r % 3)

                def down(r, i):
                    pe.wait_ge(hidden_ready, H + r + 1 + MLP_BODY * i)
                    group_down(mlp_units(U, r + 1)[1], i, r % 3, r == 0)

                up(0, 0)
                for r in range(1, MLP_FIRST):
                    up(r, 0)
                    down(r - 1, 0)
                with pe.Fori(0, MLP_TRIPS) as i:
                    for r in range(MLP_FIRST, MLP_FIRST + MLP_BODY):
                        up(r, i)
                        down(r - 1, i)
                for r in range(MLP_LAST, MG):
                    up(r, 0)
                    if r < MG - 1:
                        down(r - 1, 0)
                last_down(U + 2 * MG - 2, H + MG - 1, 3, MG - 2)

            def sb_stage(U):
                row_product(U, lambda t, c: acc[:, t, c * BANK:(c + 1) * BANK])
                for j in range(8):
                    if j >= 4:
                        pe.wait_ge(sbs["q_kept"], j - 3)
                    group_up(U + 4 + j, 0, j % 4)
                pe.wait_ge(sbs["k_kept"], 4)
                pe.wait_ge(sbs["v_kept"], 1)
                pe.wait_ge(masks_ready, 2)

                def scores(h):
                    r = slice(HD * (h % 2), HD * (h % 2) + HD)
                    z, q, k = wk[:, h % 4, :], sb_q[r, h // 2, :], sb_k[r, h // 2, :]
                    nc.tensor.matmul(z[:, 0:S], k[:, 0:P], q, start=True, stop=False, skip_group_check=True)
                    nc.tensor.matmul(z[:, S:QB], k[:, P:S], q[:, P:S], start=False, stop=False,
                                     skip_group_check=True).then_inc(sbs["z_ready"], 1)

                def tails(h):
                    pe.wait_ge(sbs["softplus_ready"], h + 1)
                    z, sp = wk[:, h % 4, :], hid[:, h % 3, :]
                    nc.tensor.matmul(z[:, 0:S], neg_tri[:, :], sp[:, 0:S], start=False, stop=False, skip_group_check=True)
                    nc.tensor.matmul(z[:, P:S], neg_ones[:, :], sp[:, S:QB], start=False, stop=False, skip_group_check=True)
                    nc.tensor.matmul(z[:, S:QB], neg_tri[:, :], sp[:, S:QB], start=False, stop=True,
                                     skip_group_check=True).then_inc(sbs["logits_ready"], 1)

                def values(h):
                    j, b = h // 2, HD * (h % 2)
                    pe.wait_ge(sbs["weights_ready"], h + 1)
                    if j >= 2 and h % 2 == 0:
                        pe.wait_ge(sbs["out_kept"], j - 1)
                    o, w = acc[b:b + HD, j % 2, :], sb_a[:, h % 3, :]
                    nc.tensor.matmul(o[:, 0:S], sb_v[:, 0, h * HD:(h + 1) * HD], w[:, 0:S], start=True, stop=False,
                                     skip_group_check=True)
                    nc.tensor.matmul(o[:, P:S], sb_v[:, 1, h * HD:(h + 1) * HD], w[:, S:QB], start=False, stop=True,
                                     skip_group_check=True).then_inc(sbs["out_ready"], 1)

                for step in range(HEADS + 5):
                    if step < HEADS:
                        if step >= 4:
                            pe.wait_ge(sbs["raw_ready"], step - 3)
                        scores(step)
                    if 0 <= step - 3 < HEADS:
                        tails(step - 3)
                    if step >= 5:
                        values(step - 5)
                pe.wait_ge(sbs["out_kept"], PAIRS)
                row_product(U + 12, lambda t, c: acc[:, t, c * BANK:(c + 1) * BANK], last=True)

            def attention(sm, qT, kT, v):

                def scores(h):
                    s = wk[:, h % 2, :]
                    if h >= 2:
                        pe.wait_ge(sm["max_ready"], h - 1)
                    if sm is mla_s and h == MLA_COPIES[1][0]:
                        pe.wait_ge(sm["k_copied"], 2)
                    nc.tensor.matmul(s[:, 0:P], qT[:, h, 0:P], kT(h)[:, 0:P], start=True, stop=True)
                    nc.tensor.matmul(s[:, P:QB], qT[:, h, P:S], kT(h), start=True, stop=True).then_inc(sm["scores_ready"], 1)

                def turn_probs(h):
                    pe.wait_ge(sm["probs_ready"], h + 1)
                    if h >= 2:
                        pe.wait_ge(sm["probs_kept"], h - 1)
                    for b in range(3):
                        mm = nc.tensor.transpose(wk[:, 2 + h % 2, b * P:(b + 1) * P], hid[:, h % 3, b * P:(b + 1) * P],
                                                 ident[:, :])
                    mm.then_inc(sm["probs_turned"], 1)

                def values(h):
                    pe.wait_ge(sm["probs_kept"], h + 1)
                    c = slice(h * HD, (h + 1) * HD)
                    p = probs_T[:, h % 2, :]
                    nc.tensor.matmul(acc[:, 0, c], p[:, 0:P], v(h, 0), start=True, stop=True)
                    nc.tensor.matmul(acc[:, 1, c], p[:, P:S], v(h, 0), start=True, stop=False)
                    nc.tensor.matmul(acc[:, 1, c], p[:, S:QB], v(h, 1), start=False, stop=True).then_inc(sm["out_ready"], 1)

                scores(0)
                scores(1)
                for h in range(HEADS):
                    if h + 2 < HEADS:
                        scores(h + 2)
                    turn_probs(h)
                    if h:
                        values(h - 1)
                values(HEADS - 1)

            def fill_free(sm, f):
                if f >= 4:
                    kept = (f - 4) // 2 + 1
                    pe.wait_ge(sm["fill_a" if f % 2 == 0 else "fill_v"], kept)

            def mla_stage(U):
                row_product(U, lambda t, c: acc[:, t, 0:MLA_IN], halves=1, n=MLA_IN)
                pe.wait_ge(mla_s["c_rows"], 1)
                for bank, col, width in ((0, 0, P), (0, P, P), (1, 2 * P, P), (2, 3 * P, MLA_W)):
                    for t in range(T):
                        at = S if (bank == 0 and col) else 0
                        mm = nc.tensor.transpose(wk[0:width, bank, at + t * P:at + (t + 1) * P],
                                                 xn[:, t, col:col + width], ident[:, :])
                    mm.then_inc(mla_s["c_turned"], 1)
                pe.wait_ge(mla_s["c_kept"], 4)
                wait_unit(U + 2)
                for u, dst, base in ((U + 2, lambda t, c: acc[:, t, c * BANK:(c + 1) * BANK], 2), (U + 3, lambda t, c: wk[:, t, :], 1)):
                    wait_unit(u)
                    wh, wl = slot(whi, u, 2), slot(wlo, u, 2)
                    for k in range(2):
                        for t in range(T):
                            r = slice(t * P, (t + 1) * P)
                            for c in range(base):
                                n = slice(c * BANK, (c + 1) * BANK)
                                mm = product(dst(t, c), (xTh[:, k, r], xTl[:, k, r]), (wh[:, k, n], wl[:, k, n]), k == 0, k == 1)
                    mm.then_inc(unit_done, 1)
                u = U + 4
                wait_unit(u)
                wh, wl = whi[:, u % RING, :], wlo[:, u % RING, :]
                for j in range(PAIRS):
                    f = 2 + j
                    fill_free(mla_s, f)
                    for e in range(2):
                        c = slice((2 * j + e) * P, (2 * j + e + 1) * P)
                        mm = product(wk[:, f % 4, e * S:(e + 1) * S], (wh[:, c], wl[:, c]), (xTh[:, 2, :], xTl[:, 2, :]), True, True)
                    mm.then_inc(mla_s["fill_ready"], 1)
                pe.wait_ge(mla_s["rows_kept_v"], 1)
                wh, wl = slot(whi, u, HEADS), slot(wlo, u, HEADS)
                for t in range(T):
                    r = slice(t * P, (t + 1) * P)
                    for c in range(2):
                        h = slice(8 * c, 8 * c + 8)
                        mm = product(acc[:, t, c * BANK:(c + 1) * BANK], (xTh[:, 2, r], xTl[:, 2, r]),
                                     (wh[:, h, NOPE:P], wl[:, h, NOPE:P]), True, True)
                mm.then_inc(unit_done, 1)
                pe.wait_ge(mla_s["roped"], 1)
                turn_heads(mla_s, 10, mla_q, HEADS, MLA_W)
                pe.wait_ge(mla_s["fill_a"], 9)
                pe.wait_ge(mla_s["fill_v"], 9)
                pe.wait_ge(mla_s["k_copied"], 1)
                pe.wait_ge(mla_s["v_kept"], 1)
                attention(mla_s, mla_qT, lambda h: mla_kT[:, h, :], lambda h, t: mla_v[:, t, h * HD:(h + 1) * HD])

            def turn_heads(sm, f0, rows, heads, width, shift=0):
                for j in range(heads // 2):
                    f = f0 + j
                    fill_free(sm, f)
                    for e in range(2):
                        for t in range(T):
                            mm = nc.tensor.transpose(wk[0:width, (f + shift) % 4, e * S + t * P:e * S + (t + 1) * P],
                                                     rows[:, t, 2 * j + e, :], ident[:, :])
                    mm.then_inc(sm["fill_ready"], 1)

            def mlstm_stage(U):
                row_product(U, lambda t, c: acc[:, t, c * BANK:(c + 1) * BANK])
                u = U + 4
                wait_unit(u)
                wh, wl = slot(whi, u, 8), slot(wlo, u, 8)
                for t in range(T):
                    r = slice(t * P, (t + 1) * P)
                    for k in range(KD):
                        mm = product(wk[:, 0, t * 8:t * 8 + 8], (xTh[:, k, r], xTl[:, k, r]),
                                     (wh[:, k, 0:8], wl[:, k, 0:8]), k == 0, k == KD - 1)
                mm.then_inc(unit_done, 1)
                pe.wait_ge(ml["o_kept"], T)
                row_product(U + 5, lambda t, c: acc[:, t, 0:BANK], halves=1)
                pe.wait_ge(ml["gates_ready"], 1)
                for j in range(2):
                    for t in range(T):
                        mm = nc.tensor.transpose(wk[0:M_HEADS, 1, j * S + t * P:j * S + (t + 1) * P],
                                                 ml_pre[:, t, j * M_HEADS:(j + 1) * M_HEADS], ident[:, :])
                mm.then_inc(ml["gates_turned"], 1)
                row_product(U + 7, lambda t, c: acc[:, t, BANK:D], halves=1)
                pe.wait_ge(ml["consts"], 2)
                pe.wait_ge(ml["m_ready"], 1)
                pe.wait_ge(ml["floor_ready"], 1)
                for j, rows in enumerate((ML_G, ML_FLOOR)):
                    for t in range(T):
                        mm = nc.tensor.transpose(wk[:, 2, 8 * j + 4 * t:8 * j + 4 * t + 4], rows[:, t * P:(t + 1) * P],
                                                 ident[0:M_HEADS, 0:M_HEADS])
                mm.then_inc(ml["cols_turned"], 1)
                for h in range(M_HEADS):
                    mm = nc.tensor.matmul(wk[:, (3, 0)[h // 2], (h % 2) * S:(h % 2 + 1) * S],
                                          ml_select[:, h * P:(h + 1) * P], ML_M, start=True, stop=True)
                    if h % 2:
                        mm.then_inc(ml["spread"], 1)
                for j, bank in enumerate((1, 2, 3, 0)):
                    if j == 1:
                        pe.wait_ge(ml["cols_kept"], 1)
                    if j >= 2:
                        pe.wait_ge(ml["bounded"], 2 * (j - 1))
                    group_up(U + 9 + j, 0, bank)
                pe.wait_ge(ml["q_kept"], 2)
                pe.wait_ge(ml["k_kept"], 2)

                def scores(h):
                    z, q, k = wk[:, h, :], ml_q[:, h, :], ml_k[:, h, :]
                    nc.tensor.matmul(z[:, 0:S], k[:, 0:P], q, start=True, stop=True)
                    nc.tensor.matmul(z[:, S:QB], k[:, P:S], q[:, P:S], start=True, stop=True).then_inc(ml["scores_ready"], 1)

                def outputs(h):
                    pe.wait_ge(ml["weights_ready"], h + 1)
                    w = ml_scores[:, h, :]
                    for rhs, dst in ((lambda t: ml_v[:, t, h * M_DV:(h + 1) * M_DV], lambda t: acc[:, t, h * M_DV:(h + 1) * M_DV]),
                                     (lambda t: neg_ones[:, 0:1], lambda t: wk[:, h, QB + t:QB + t + 1])):
                        nc.tensor.matmul(dst(0), w[:, 0:P], rhs(0), start=True, stop=True)
                        nc.tensor.matmul(dst(1), w[:, P:S], rhs(0), start=True, stop=False)
                        mm = nc.tensor.matmul(dst(1), w[:, S:QB], rhs(1), start=False, stop=True)
                    mm.then_inc(ml["out_ready"], 1)

                for h in range(M_HEADS):
                    scores(h)
                pe.wait_ge(ml["v_kept"], 1)
                for h in range(M_HEADS):
                    outputs(h)

            def swa_stage(U):
                pe.wait_ge(turned_kept, KD // 2 * fresh[0] + T)
                row_product(U, lambda t, c: wk[:, t, :], halves=1)
                row_product(U + 2, lambda t, c: acc[:, t, c * BANK:(c + 1) * BANK])
                k = swa_kv[:, :, 0:KV_HEADS * HD].rearrange("p t (h w) -> p t h w", w=HD)
                pe.wait_ge(swa_s["roped"], 1)
                turn_heads(swa_s, 0, k, KV_HEADS, HD, 2)
                pe.wait_ge(swa_s["roped"], 2)
                pe.wait_ge(swa_s["roped_v"], 1)
                turn_heads(swa_s, 2, swa_q, HEADS, HD, 2)
                pe.wait_ge(swa_s["fill_a"], 5)
                pe.wait_ge(swa_s["fill_v"], 5)
                group = HEADS // KV_HEADS
                attention(swa_s, swa_qT, lambda h: swa_kT[:, h // group, :],
                          lambda h, t: swa_kv[:, t, (KV_HEADS + h // group) * HD:(KV_HEADS + h // group + 1) * HD])

            def ple_stage(U, n, m, s):
                pe.wait_ge(p_loaded, 16 * (n + 1))
                for k in range(2):
                    for t in range(T):
                        mm = nc.tensor.transpose(wk[:, 0, k * S + t * P:k * S + (t + 1) * P],
                                                 ple_rows[:, t, k * P:(k + 1) * P], ident[:, :])
                mm.then_inc(ple_s["turned"], 1)
                pe.wait_ge(ple_s["kept"], n + 1)
                turn(m, x, lambda t: (x_ready, T * s - 1 + t))
                row_product(U, lambda t, c: acc[:, t, c * BANK:(c + 1) * BANK], last=True)
                u = U + 4
                wait_unit(u)
                wh, wl = slot(whi, u, 2), slot(wlo, u, 2)
                for t in range(T):
                    r = slice(t * P, (t + 1) * P)
                    for k in range(2):
                        for c in range(2):
                            q = slice(c * BANK, (c + 1) * BANK)
                            mm = product(wk[:, 2 * t + c, :], (hTh[:, 0, k, r], hTl[:, 0, k, r]),
                                         (wh[:, k, q], wl[:, k, q]), k == 0, k == 1)
                    mm.then_inc(unit_done if t else ple_s["projected"], 1)

            pe.wait_ge(ident_ready, 1)
            pe.wait_ge(gains_loaded, 48)
            nc.tensor.transpose(wk[:, 3, 0:NG], gain_rows[:, :], ident[0:NG, 0:NG]).then_inc(gains_turned, 1)
            pe.wait_ge(pos_made, 1)
            nc.tensor.transpose(wk[:, 2, 0:4], pos_rows[:, :], ident[0:4, 0:4]).then_inc(pos_turned, 1)
            pe.wait_ge(gains_kept, 2)
            m = rows = hidden = outs = 0
            for s, (name, U, n) in enumerate(plan):
                if name in ("ffn", "sb", "mla"):
                    turn(m, x, lambda t: (scales_ready, T * rows + t + 1), scaled=True)
                    m, rows = m + 1, rows + 1
                if name == "ffn":
                    ffn(U, hidden)
                    hidden += FG
                if name == "sb":
                    sb_stage(U)
                if name == "mla":
                    mla_stage(U)
                if name in ("mlstm", "mlp", "swa"):
                    turn(m, x, lambda t: (x_ready, T * s - 1 + t))
                    m += 1
                if name == "mlp":
                    mlp(U, hidden)
                    hidden += MG
                if name == "mlstm":
                    mlstm_stage(U)
                if name == "swa":
                    swa_stage(U)
                if name == "ple":
                    ple_stage(U, n, m, s)
                    m += 1
                if name in ("mla", "mlstm", "swa"):
                    turn(m, xn, lambda t: (mixed, T * outs + t + 1))
                    m, outs = m + 1, outs + 1
                    row_product(U + STAGE_UNITS[name] - 4, lambda t, c: acc[:, t, c * BANK:(c + 1) * BANK], last=True)

        @block.scalar
        def _(act):
            chain = Chain(act, act_chain)
            A = nc.scalar.activation
            next_unit = [0]

            def split(u, i=0):
                act.wait_ge(landed[u % RING], 16 * (u // RING + 1) + 16 * (LOOP_UNITS // RING) * i)
                if u >= RING:
                    act.wait_ge(unit_done, u - RING + 1 + LOOP_UNITS * i)
                A(whi[:, u % RING, :], raw[:, u % RING, :], ACT.Copy).then_inc(high_ready, 1)

            def split_to(u):
                while next_unit[0] < min(u, TOTAL):
                    split(next_unit[0])
                    next_unit[0] += 1

            def root_mean_square(src, t, at, half=False):
                chain.link(A(square_out[:, t, :], src, ACT.Square, accum_out=stat[:, at:at + 1]))
                A(stat[:, at + 2:at + 3], stat[:, at:at + 1], ACT.Sqrt, scale=(4.0 if half else 1.0) / D,
                  bias=eps[:, 1:2] if half else eps[:, 0:1]).then_inc(std_ready, 1)

            def keep_turned(m, gain):
                for b in range(KD // 2):
                    act.wait_ge(turned, KD // 2 * m + b + 1)
                    if gain is None:
                        A(xTh[:, 2 * b:2 * b + 2, :].rearrange("p k s -> p (k s)"), wk[:, b, :],
                          ACT.Copy).then_inc(turned_high, 1)
                    else:
                        for k in (2 * b, 2 * b + 1):
                            ins = A(xTh[:, k, :], wk[:, b, (k % 2) * S:(k % 2 + 1) * S], ACT.Copy,
                                    scale=gain[:, k:k + 1])
                        ins.then_inc(turned_high, 1)

            def rms_in(s, m, U, gain):
                for t in range(T):
                    if s == 0:
                        act.wait_ge(x_loaded[t], 16)
                    else:
                        act.wait_ge(x_ready, T * s - 1 + t)
                    root_mean_square(x[:, t, :], t, 4 + t)
                    if s:
                        split_to(U + 2 + t)
                split_to(U + (RING if s else 1))
                if s == 0:
                    act.wait_ge(gains_kept, 1)
                keep_turned(m, gain)
                split_to(U + RING)

            def hidden_step(H, r, i, body, bank, buffer, func, gate, up, down, last):
                h = H + r
                act.wait_ge(unit_done, gate + 1 + LOOP_UNITS * i)
                back = body if body == 3 else 2
                if h - back + 1 > 0:
                    act.wait_ge(hidden_ready, h - back + 1 + body * i)
                A(hid[:, buffer, :], wk[:, bank, :], func).then_inc(act_ready, 1)
                if up is not None:
                    split(gate + 3, i)
                newest = (up if up is not None else gate) + 3
                if not last:
                    split(newest, i)
                act.wait_ge(hidden_made, h + 1 + body * i)
                A(hTh[:, buffer].rearrange("p k s -> p (k s)"), hid[:, buffer, :], ACT.Copy).then_inc(hidden_high, 1)
                if last:
                    split(newest, i)
                if down is not None:
                    split(down + 3, i)

            def ffn(U, H):
                def step(r, i):
                    gate, up, down = ffn_units(U, r)
                    hidden_step(H, r, i, FFN_BODY, 2 * (r % 2), r % 2, ACT.Silu, gate, up, down if 0 < r < FG - 1 else None, r == FG - 1)
                split_to(U + RING)
                for r in range(FFN_FIRST):
                    step(r, 0)
                with act.Fori(0, FFN_TRIPS) as i:
                    for r in range(FFN_FIRST, FFN_FIRST + FFN_BODY):
                        step(r, i)
                for r in range(FFN_LAST, FG):
                    step(r, 0)
                next_unit[0] = U + 3 * FG + 1

            def mlp(U, H):
                def step(r, i):
                    up, down = mlp_units(U, r)
                    hidden_step(H, r, i, MLP_BODY, r % 3, r % 3, ACT.Relu, up, None, down if 0 < r < MG - 1 else None, r == MG - 1)
                split_to(U + RING)
                for r in range(MLP_FIRST):
                    step(r, 0)
                with act.Fori(0, MLP_TRIPS) as i:
                    for r in range(MLP_FIRST, MLP_FIRST + MLP_BODY):
                        step(r, i)
                for r in range(MLP_LAST, MG):
                    step(r, 0)
                next_unit[0] = U + 2 * MG + 1

            def sb_stage(U):
                for j in range(12):
                    if j >= 8:
                        act.wait_ge(unit_done, U + j + 1)
                        A(sb_k[:, 2 * (j - 8):2 * (j - 7), :].rearrange("p j s -> p (j s)"), wk[:, j - 8, :],
                          ACT.Copy).then_inc(sbs["k_kept"], 1)
                    split_to(min(U + RING + j + 1, U + 13))

                def logs(h):
                    act.wait_ge(sbs["abs_ready"], h + 1)
                    e = hid[:, h % 3, 0:QB]
                    chain.link(A(e, e, ACT.Exp, scale=-1.0))
                    A(e, e, ACT.Ln, bias=1.0).then_inc(sbs["log_ready"], 1)

                act.preload_act_table_set("natural_log_exp_and_others")
                for step in range(HEADS + 6):
                    h = step - 3
                    if 0 <= h < HEADS:
                        act.wait_ge(sbs["logits_ready"], h + 1)
                        if h >= 3:
                            act.wait_ge(sbs["out_ready"], h - 2)
                        A(sb_a[:, h % 3, :], wk[:, h % 4, 0:QB], ACT.Exp).then_inc(sbs["raw_ready"], 1)
                    if step < HEADS:
                        logs(step)
                    if step >= 7 and step % 2:
                        pair_high((step - 7) // 2)
                split_to(U + 16)

            def pair_high(j):
                act.wait_ge(sbs["out_ready"], 2 * j + 2)
                A(xTh[:, j, :], acc[:, j % 2, 0:S], ACT.Copy).then_inc(sbs["out_high"], 1)

            def keep_fills(sm, fills, first, dst, width, shift=0):
                for f in fills:
                    if f % 2 == 0:
                        act.wait_ge(sm["fill_ready"], f - first + 1)
                        j = f - fills[0]
                        A(dst[0:width, 2 * j:2 * j + 2, :], wk[0:width, (f + shift) % 4, :].rearrange(
                            "p (e s) -> p e s", e=2), ACT.Copy).then_inc(sm["fill_a"], 1)

            def attention(sm, sink):
                def keep_probs(h):
                    act.wait_ge(sm["probs_turned"], h + 1)
                    if h >= 2:
                        act.wait_ge(sm["out_ready"], h - 1)
                    A(probs_T[:, h % 2, :], wk[:, 2 + h % 2, 0:QB], ACT.Copy).then_inc(sm["probs_kept"], 1)

                act.preload_act_table_set("natural_log_exp_and_others")
                for h in range(HEADS):
                    act.wait_ge(sm["max_ready"], h + 1)
                    for t, c in ((0, slice(0, P)), (1, slice(P, QB))):
                        e, at = hid[:, h % 3, c], 2 * h + t
                        ins = A(e, e, ACT.Exp, bias=att_stat[:, NMAX, at:at + 1], accum_out=att_stat[:, SUMS, at:at + 1])
                    ins.then_inc(sm["probs_ready"], 1)
                    if h:
                        keep_probs(h - 1)
                    if sink and h in (8, HEADS - 1):
                        c = slice(0, HEADS) if h == 8 else slice(HEADS, 2 * HEADS)
                        act.wait_ge(sm["sum_read"], (h + 1) // 8)
                        A(att_stat[:, SMALL, c], att_stat[:, SINKX, c], ACT.Exp).then_inc(sm["sink_exp"], 1)
                keep_probs(HEADS - 1)

            def mla_stage(U):
                split_to(U + 4)
                act.wait_ge(unit_done, U + 2)
                for j, (t, c) in enumerate([(t, c) for c in (slice(0, Q_LORA), slice(Q_LORA, Q_LORA + KV_LORA)) for t in range(T)]):
                    ins = A(square_out[:, t, c], acc[:, t, c], ACT.Square, accum_out=stat[:, 16 + j:17 + j])
                    if j < 3:
                        chain.count(ins)
                chain.link(ins)
                for c, width in ((16, Q_LORA), (18, KV_LORA)):
                    A(stat[:, c + 4:c + 6], stat[:, c:c + 2], ACT.Sqrt, scale=1.0 / width,
                      bias=eps[:, 0:1]).then_inc(mla_s["squares"], 1)
                split_to(U + 5)
                act.wait_ge(mla_s["c_turned"], 2)
                A(xTh[:, 0, :], wk[:, 0, 0:S], ACT.Copy, scale=gain_cols[:, 96:97])
                A(xTh[:, 1, :], wk[:, 0, S:2 * S], ACT.Copy, scale=gain_cols[:, 97:98]).then_inc(mla_s["c_high"], 1)
                act.wait_ge(mla_s["c_turned"], 3)
                A(xTh[:, 2, :], wk[:, 1, 0:S], ACT.Copy, scale=gain_cols[:, 98:99]).then_inc(mla_s["c_high"], 1)
                act.wait_ge(unit_done, U + 4)
                A(work[:, D:D + BANK], wk[:, 0, :], ACT.Copy).then_inc(mla_s["fill_a"], 1)
                keep_fills(mla_s, range(2, 10), 2, mla_kT, NOPE)
                split_to(U + 6)
                keep_fills(mla_s, range(10, 18), 2, mla_qT, MLA_W)
                attention(mla_s, False)

            def mlstm_stage(U):
                split_to(U + 7)
                act.wait_ge(unit_done, U + 4)
                for t in range(T):
                    A(ml_gate[:, t, :], acc[:, t, :], ACT.Sigmoid).then_inc(ml["o_kept"], 1)
                split_to(U + 8)
                act.wait_ge(ml["biased"], 1)
                A(ml_small[:, 0:16], ml_small[:, 0:16], ACT.Tanh, scale=1.0 / GATE_CAP).then_inc(ml["tanh"], 1)
                act.wait_ge(ml["abs"], 1)
                act.preload_act_table_set("natural_log_exp_and_others")
                chain.link(A(ml_small[:, 16:24], ml_small[:, 16:24], ACT.Exp, scale=-1.0))
                A(ml_small[:, 16:24], ml_small[:, 16:24], ACT.Ln, bias=1.0).then_inc(ml["log"], 1)
                split_to(U + 10)
                act.wait_ge(ml["m_ready"], 1)
                A(ML_FLOOR, ML_FLOOR, ACT.Exp, scale=-1.0).then_inc(ml["floor_ready"], 1)
                split_to(U + 12)
                for h in range(M_HEADS):
                    act.wait_ge(ml["bounded"], h + 1)
                    A(ml_decay[:, h, :], ml_decay[:, h, :], ACT.Exp).then_inc(ml["decay_ready"], 1)
                split_to(U + 13)
                for j in range(2):
                    act.wait_ge(unit_done, U + 10 + j)
                    A(ml_q[:, 2 * j:2 * j + 2, :].rearrange("p h s -> p (h s)"), wk[:, 1 + j, :], ACT.Copy,
                      scale=M_DK ** -0.5).then_inc(ml["q_kept"], 1)
                    split_to(U + 14)
                act.preload_act_table_set("sqrt_and_others")
                act.wait_ge(ml["var_ready"], 1)
                A(ml_half, ml_var, ACT.Sqrt, bias=eps[:, 2:3]).then_inc(ml["dev_ready"], 1)

            def swa_stage(U):
                split_to(U + 7)
                keep_fills(swa_s, range(0, 2), 0, swa_kT, HD, 2)
                keep_fills(swa_s, range(2, 10), 0, swa_qT, HD, 2)
                attention(swa_s, True)

            def ple_stage(U, n, m):
                act.wait_ge(ple_s["turned"], n + 1)
                A(hTh[:, 0].rearrange("p k s -> p (k s)"), wk[:, 0, :], ACT.Copy).then_inc(ple_s["high"], 1)
                split_to(U + RING)
                keep_turned(m, None)
                split_to(U + 6)
                act.preload_act_table_set("sigmoid_and_others")
                for t in range(T):
                    act.wait_ge(ple_s["biased"], T * n + t + 1)
                    A(xn[:, t, :], xn[:, t, :], ACT.Sigmoid).then_inc(ple_s["gate"], 1)

            m = hidden = norms = 0
            act.preload_act_table_set("sqrt_and_others")
            act.wait_ge(eps_ready, 3)
            for s, (name, U, n) in enumerate(plan):
                if name in ("ffn", "sb", "mla"):
                    col = {"ffn": (6 * (n // 2) + 4 * (n % 2)), "sb": 2, "mla": 8}[name] * KD
                    rms_in(s, m, U, gain_cols[:, col:col + KD])
                    m += 1
                if name == "ffn":
                    ffn(U, hidden)
                    hidden += FG
                if name == "sb":
                    sb_stage(U)
                if name == "mla":
                    mla_stage(U)
                if name in ("mlstm", "mlp", "swa"):
                    split_to(U + RING)
                    keep_turned(m, None)
                    m += 1
                if name == "mlp":
                    mlp(U, hidden)
                    hidden += MG
                if name == "mlstm":
                    mlstm_stage(U)
                if name == "swa":
                    swa_stage(U)
                if name == "ple":
                    ple_stage(U, n, m)
                    m += 1
                if name in ("mla", "mlstm", "swa"):
                    keep_turned(m, None)
                    m += 1
                    split_to(U + STAGE_UNITS[name] + 1)
                if name in ("ffn", "sb", "mla"):
                    if s == 0:
                        act.wait_ge(angles_ready, 1)
                        A(trig[:, :], angle[:, :], ACT.Sin).then_inc(trig_ready, 1)
                    act.preload_act_table_set("sqrt_and_others")
                    act.wait_ge(result, s + 1)
                    root_mean_square(acc[:, 0, :], 0, 0, name == "ffn")
                    act.wait_ge(unit_done, U + STAGE_UNITS[name])
                    root_mean_square(acc[:, 1, :], 1, 1, name == "ffn")
                if name in ("mlstm", "mlp", "swa"):
                    act.preload_act_table_set("sqrt_and_others")
                    for t in range(T):
                        act.wait_ge(var_ready, T * norms + t + 1)
                        A(stat[:, 2 + t:3 + t], stat[:, 11 + 2 * t:12 + 2 * t], ACT.Sqrt,
                          bias=eps[:, 2:3]).then_inc(dev_ready, 1)
                        if t == 0:
                            split_to(U + STAGE_UNITS[name] + 2)
                    norms += 1

        @block.vector
        def _(dve):
            chain = Chain(dve, dve_chain)
            V = nc.vector
            next_unit = [0]

            def split(u, i=0):
                dve.wait_ge(high_ready, u + 1 + LOOP_UNITS * i)
                V.tensor_tensor(wlo[:, u % RING, :], raw[:, u % RING, :], whi[:, u % RING, :].bitcast(F32),
                                ALU.subtract).then_inc(unit_ready, 1)

            def split_to(u):
                while next_unit[0] < min(u, TOTAL):
                    split(next_unit[0])
                    next_unit[0] += 1

            def keep_turned(m, gain):
                for b in range(KD // 2):
                    dve.wait_ge(turned_high, KD // 2 * m + b + 1)
                    if gain is None:
                        V.tensor_tensor(xTl[:, 2 * b:2 * b + 2, :].rearrange("p k s -> p (k s)"), wk[:, b, :],
                                        xTh[:, 2 * b:2 * b + 2, :].rearrange("p k s -> p (k s)").bitcast(F32),
                                        ALU.subtract).then_inc(turned_kept, 1)
                    else:
                        for k in (2 * b, 2 * b + 1):
                            ins = V.scalar_tensor_tensor(xTl[:, k, :], wk[:, b, (k % 2) * S:(k % 2 + 1) * S],
                                                         gain[:, k:k + 1], xTh[:, k, :].bitcast(F32),
                                                         ALU.mult, ALU.subtract)
                        ins.then_inc(turned_kept, 1)

            def rms_in(scaled, m, U, gain):
                for t in range(T):
                    dve.wait_ge(std_ready, scaled + t + 1)
                    y = stat[:, 32 + t:33 + t]
                    chain.link(V.reciprocal(y, stat[:, 6 + t:7 + t]))
                    V.tensor_scalar(scales[:, t, :], ident[:, :], y, None, ALU.mult).then_inc(scales_ready, 1)
                if m == 0:
                    split_to(U + 1)
                keep_turned(m, gain)
                split_to(U + RING)

            def wait_result(s, end, t):
                if t == 0:
                    dve.wait_ge(result, s + 1)
                else:
                    dve.wait_ge(unit_done, end)

            def rms_out(scaled, nv):
                dve.wait_ge(vec_loaded[nv % 3], 16 * (nv // 3 + 1))
                for t in range(T):
                    dve.wait_ge(std_ready, scaled + t + 1)
                    r = stat[:, 8 + t:9 + t]
                    chain.link(V.reciprocal(r, stat[:, 2 + t:3 + t]))
                    chain.link(V.scalar_tensor_tensor(xn[:, t, :], acc[:, t, :], r, vec[:, nv % 3, :], ALU.mult, ALU.mult))
                    V.tensor_tensor(x[:, t, :], x[:, t, :], xn[:, t, :], ALU.add).then_inc(x_ready, 1)

            def hidden_step(H, r, i, body, bank, buffer, gate, up, down, last):
                h = H + r
                if up is not None:
                    split(gate + 3, i)
                    dve.wait_ge(unit_done, up + 1 + LOOP_UNITS * i)
                dve.wait_ge(act_ready, h + 1 + body * i)
                e = hid[:, buffer, :]
                V.tensor_tensor(e, e, wk[:, bank, :], ALU.mult).then_inc(hidden_made, 1)
                newest = (up if up is not None else gate) + 3
                if not last:
                    split(newest, i)
                dve.wait_ge(hidden_high, h + 1 + body * i)
                V.tensor_tensor(hTl[:, buffer].rearrange("p k s -> p (k s)"), e,
                                hTh[:, buffer].rearrange("p k s -> p (k s)").bitcast(F32),
                                ALU.subtract).then_inc(hidden_ready, 1)
                if last:
                    split(newest, i)
                if down is not None:
                    split(down + 3, i)

            def ffn(U, H):
                def step(r, i):
                    gate, up, down = ffn_units(U, r)
                    hidden_step(H, r, i, FFN_BODY, 2 * (r % 2) + 1, r % 2, gate, up, down if 0 < r < FG - 1 else None, r == FG - 1)
                split_to(U + RING)
                for r in range(FFN_FIRST):
                    step(r, 0)
                with dve.Fori(0, FFN_TRIPS) as i:
                    for r in range(FFN_FIRST, FFN_FIRST + FFN_BODY):
                        step(r, i)
                for r in range(FFN_LAST, FG):
                    step(r, 0)
                next_unit[0] = U + 3 * FG + 1

            def mlp(U, H):
                def step(r, i):
                    up, down = mlp_units(U, r)
                    hidden_step(H, r, i, MLP_BODY, r % 3, r % 3, up, None, down if 0 < r < MG - 1 else None, r == MG - 1)
                split_to(U + RING)
                for r in range(MLP_FIRST):
                    step(r, 0)
                with dve.Fori(0, MLP_TRIPS) as i:
                    for r in range(MLP_FIRST, MLP_FIRST + MLP_BODY):
                        step(r, i)
                for r in range(MLP_LAST, MG):
                    step(r, 0)
                next_unit[0] = U + 2 * MG + 1

            def sb_stage(U):
                for j in range(12):
                    if j == 3:
                        dve.wait_ge(unit_done, U + 4)
                        for t in range(T):
                            ins = V.tensor_copy(sb_v[:, t, :], acc[:, t, :])
                        ins.then_inc(sbs["v_kept"], 1)
                    if 4 <= j < 8:
                        dve.wait_ge(unit_done, U + j + 1)
                        V.tensor_scalar(sb_q[:, 2 * (j - 4):2 * (j - 3), :].rearrange("p j s -> p (j s)"), wk[:, j - 4, :],
                                        HD ** -0.5, None, ALU.mult).then_inc(sbs["q_kept"], 1)
                    split_to(min(U + RING + j + 1, U + 13))

                def absolute(h):
                    dve.wait_ge(sbs["z_ready"], h + 1)
                    if h >= 3:
                        dve.wait_ge(sbs["logits_ready"], h - 2)
                    V.tensor_scalar(hid[:, h % 3, 0:QB].bitcast(I32), wk[:, h % 4, 0:QB].bitcast(I32), 0x7fffffff, None,
                                    ALU.bitwise_and).then_inc(sbs["abs_ready"], 1)

                def softplus(h):
                    dve.wait_ge(sbs["log_ready"], h + 1)
                    e = hid[:, h % 3, 0:QB]
                    chain.link(V.scalar_tensor_tensor(e, wk[:, h % 4, 0:QB], 0.0, e, ALU.max, ALU.add))
                    V.tensor_tensor(diagonal(e), diagonal(e), later[:, :].unsqueeze(1).broadcast_to([P, 2, P]),
                                    ALU.mult).then_inc(sbs["softplus_ready"], 1)

                def pair_low(j):
                    dve.wait_ge(sbs["out_high"], j + 1)
                    V.tensor_tensor(xTl[:, j, :], acc[:, j % 2, 0:S], xTh[:, j, :].bitcast(F32),
                                    ALU.subtract).then_inc(sbs["out_kept"], 1)

                dve.wait_ge(masks_ready, 2)
                for step in range(HEADS + 6):
                    if 0 <= step - 2 < HEADS:
                        softplus(step - 2)
                    if step < HEADS:
                        absolute(step)
                    if step >= 7 and step % 2:
                        pair_low((step - 7) // 2)
                split_to(U + 16)

            def keep_fills(sm, fills, first, dst, width, shift=0):
                for f in fills:
                    if f % 2:
                        dve.wait_ge(sm["fill_ready"], f - first + 1)
                        j = f - fills[0]
                        V.tensor_copy(dst[0:width, 2 * j:2 * j + 2, :], wk[0:width, (f + shift) % 4, :].rearrange(
                            "p (e s) -> p e s", e=2)).then_inc(sm["fill_v"], 1)

            def attention(sm, scale, bias, sink, mixed_before):
                def maxima(h):
                    dve.wait_ge(sm["scores_ready"], h + 1)
                    if h >= 3:
                        dve.wait_ge(sm["probs_turned"], h - 2)
                    e = hid[:, h % 3, 0:QB]
                    chain.link(V.scalar_tensor_tensor(e, wk[:, h % 2, 0:QB], scale, bias[:, :], ALU.mult, ALU.add))
                    both = att_stat[:, NMAX, 2 * h:2 * h + 2]
                    ins = V.tensor_reduce(both[:, 0:1], e[:, 0:P], AX.X, ALU.max, negate=True)
                    if sink:
                        chain.count(ins)
                    ins = V.tensor_reduce(both[:, 1:2], e[:, P:QB], AX.X, ALU.max, negate=True)
                    if sink:
                        chain.link(ins)
                        ins = V.tensor_scalar(both, both, minus_sinks[:, h:h + 1], None, ALU.min)
                    ins.then_inc(sm["max_ready"], 1)

                def sink_terms(c):
                    n = slice(HEADS * c, HEADS * c + HEADS)
                    dve.wait_ge(sm["max_ready"], 8 * c + 8)
                    V.tensor_tensor(att_stat[:, SINKX, n].rearrange("p (h t) -> p h t", t=T),
                                    att_stat[:, NMAX, n].rearrange("p (h t) -> p h t", t=T),
                                    sinks[:, 8 * c:8 * c + 8].unsqueeze(2).broadcast_to([P, 8, T]),
                                    ALU.add).then_inc(sm["sum_read"], 1)

                def outputs(c):
                    dve.wait_ge(sm["out_ready"], 8 * c + 8)
                    n = slice(HEADS * c, HEADS * c + HEADS)
                    if sink:
                        dve.wait_ge(sm["sink_exp"], c + 1)
                        chain.link(V.tensor_tensor(att_stat[:, SUMS, n], att_stat[:, SUMS, n], att_stat[:, SMALL, n], ALU.add))
                    chain.link(V.reciprocal(att_stat[:, RECIP, n], att_stat[:, SUMS, n]))
                    r = att_stat[:, RECIP, n].rearrange("p (h t) -> p h t", t=T)
                    for t in range(T):
                        ins = V.tensor_tensor(xn[:, t, c * BANK:(c + 1) * BANK].rearrange("p (h w) -> p h w", w=HD),
                                              acc[:, t, c * BANK:(c + 1) * BANK].rearrange("p (h w) -> p h w", w=HD),
                                              r[:, :, t:t + 1].broadcast_to([P, 8, HD]), ALU.mult)
                        if c:
                            ins.then_inc(mixed, 1)

                for h in range(HEADS):
                    maxima(h)
                    if h in (7, 15) and sink:
                        sink_terms(h // 8)
                    if h == 11:
                        outputs(0)
                outputs(1)

            def mla_stage(U, outs):
                split_to(U + 4)
                dve.wait_ge(mla_s["squares"], 2)
                chain.link(V.reciprocal(stat[:, 28:32], stat[:, 20:24]))
                chain.count(V.memset(xn[:, :, 3 * P:3 * P + NOPE], 0.0))
                for t in range(T):
                    chain.count(V.tensor_scalar(xn[:, t, 0:Q_LORA], acc[:, t, 0:Q_LORA], stat[:, 28 + t:29 + t], None, ALU.mult))
                    chain.count(V.tensor_scalar(xn[:, t, Q_LORA:3 * P], acc[:, t, Q_LORA:3 * P], stat[:, 30 + t:31 + t],
                                                None, ALU.mult))
                k = xn[:, :, 3 * P + NOPE:3 * P + MLA_W]
                chain.link(V.tensor_copy(k, acc[:, :, 3 * P:MLA_IN]))
                dve.wait_ge(trig_ready, 1)
                rope(V, chain, k.unsqueeze(2), sin1, cos1, ROPE // 2).then_inc(mla_s["c_rows"], 1)
                split_to(U + 5)
                dve.wait_ge(mla_s["c_high"], 1)
                for k, at in ((0, 0), (1, S)):
                    V.scalar_tensor_tensor(xTl[:, k, :], wk[:, 0, at:at + S], gain_cols[:, 96 + k:97 + k],
                                           xTh[:, k, :].bitcast(F32), ALU.mult, ALU.subtract).then_inc(mla_s["c_kept"], 1)
                dve.wait_ge(mla_s["c_high"], 2)
                V.scalar_tensor_tensor(xTl[:, 2, :], wk[:, 1, 0:S], gain_cols[:, 98:99],
                                       xTh[:, 2, :].bitcast(F32), ALU.mult, ALU.subtract).then_inc(mla_s["c_kept"], 1)
                dve.wait_ge(mla_s["c_turned"], 4)
                V.tensor_copy(mla_kT[NOPE:MLA_W, 0, :], wk[NOPE:MLA_W, 2, 0:S]).then_inc(mla_s["c_kept"], 1)
                dve.wait_ge(unit_done, U + 4)
                V.tensor_copy(work[:, 1536 + D:1536 + D + BANK], wk[:, 1, :]).then_inc(mla_s["fill_v"], 1)
                for t in range(T):
                    ins = V.tensor_copy(work[:, 1536 * t:1536 * t + D], acc[:, t, :])
                ins.then_inc(mla_s["rows_kept_v"], 1)
                keep_fills(mla_s, range(2, 10), 2, mla_kT, NOPE)
                split_to(U + 6)
                dve.wait_ge(unit_done, U + 5)
                for t in range(T):
                    ins = V.tensor_copy(mla_v[:, t, :], acc[:, t, :])
                ins.then_inc(mla_s["v_kept"], 1)
                keep_fills(mla_s, range(10, 18), 2, mla_qT, MLA_W)
                dve.wait_ge(bias_ready, 3)
                attention(mla_s, MLA_W ** -0.5, causal, False, outs)

            def mlstm_stage(U):
                split_to(U + 8)
                dve.wait_ge(ml["bias_loaded"], 32)
                dve.wait_ge(unit_done, U + 5)
                V.tensor_tensor(ml_pre, wk[:, 0, 0:16].rearrange("p (t n) -> p t n", t=T),
                                gate_bias[:, :].unsqueeze(1).broadcast_to([P, T, 8]), ALU.add).then_inc(ml["biased"], 1)
                dve.wait_ge(ml["tanh"], 1)
                chain.link(V.tensor_scalar(ml_small[:, 0:16], ml_small[:, 0:16], GATE_CAP, None, ALU.mult))
                forget = ml_pre[:, :, M_HEADS:8]
                V.tensor_scalar(ml_log.bitcast(I32), forget.bitcast(I32), 0x7fffffff, None,
                                ALU.bitwise_and).then_inc(ml["abs"], 1)
                dve.wait_ge(ml["log"], 1)
                V.scalar_tensor_tensor(forget, forget, 0.0, ml_log, ALU.min, ALU.subtract).then_inc(ml["gates_ready"], 1)
                chain.link(V.memset(ML_ONES, 1.0))
                split_to(U + 10)
                dve.wait_ge(ml["gates_turned"], 1)
                chain.link(V.tensor_tensor_scan(ML_F, ML_ONES, wk[0:M_HEADS, 1, S:2 * S], 0.0, ALU.mult, ALU.add))
                chain.link(V.tensor_tensor(ML_G, wk[0:M_HEADS, 1, 0:S], ML_F, ALU.subtract))
                chain.link(V.tensor_tensor_scan(ML_M, ML_G, ML_G, 0.0, ALU.max, ALU.max))
                V.tensor_tensor(ML_FLOOR, ML_F, ML_M, ALU.add).then_inc(ml["m_ready"], 1)
                split_to(U + 12)
                dve.wait_ge(ml["cols_turned"], 1)
                V.tensor_copy(ml_small[:, 32:48], wk[:, 2, 0:16]).then_inc(ml["cols_kept"], 1)
                dve.wait_ge(ml["cols_kept"], 1)
                for h in range(M_HEADS):
                    dve.wait_ge(ml["spread"], h // 2 + 1)
                    minus_m = wk[:, (3, 0)[h // 2], (h % 2) * S:(h % 2 + 1) * S]
                    e = ml_decay[:, h, :]
                    V.scalar_tensor_tensor(e[:, 0:S], minus_m, ml_cols[:, 0, 0, h:h + 1], ml_bound[:, 0:S], ALU.add, ALU.min)
                    V.scalar_tensor_tensor(e[:, S:QB], minus_m[:, P:S], ml_cols[:, 0, 1, h:h + 1], ml_bound[:, S:QB],
                                           ALU.add, ALU.min).then_inc(ml["bounded"], 1)
                split_to(U + 13)
                dve.wait_ge(unit_done, U + 9)
                for t in range(T):
                    ins = V.tensor_copy(ml_v[:, t, :], acc[:, t, :])
                ins.then_inc(ml["v_kept"], 1)
                split_to(U + 14)
                for j in range(2):
                    dve.wait_ge(unit_done, U + 12 + j)
                    V.tensor_copy(ml_k[:, 2 * j:2 * j + 2, :].rearrange("p h s -> p (h s)"),
                                  wk[:, (3, 0)[j], :]).then_inc(ml["k_kept"], 1)
                for h in range(M_HEADS):
                    dve.wait_ge(ml["decay_ready"], h + 1)
                    dve.wait_ge(ml["scores_ready"], h + 1)
                    V.tensor_tensor(ml_scores[:, h, :], wk[:, h, 0:QB], ml_decay[:, h, :],
                                    ALU.mult).then_inc(ml["weights_ready"], 1)
                for t in range(T):
                    dve.wait_ge(ml["gated"], t + 1)
                for h in range(M_HEADS):
                    c = slice(h * M_DV, (h + 1) * M_DV)
                    if h % 2 == 0:
                        dve.wait_ge(ml["out_ready"], h + 2)
                        for j in range(T * h, T * h + 4):
                            chain.count(V.bn_stats(ml_small[:, 48 + 6 * j:54 + 6 * j],
                                                   acc[:, j % T, (j // T) * M_DV:(j // T + 1) * M_DV]))
                        if h:
                            den = ml_inv.rearrange("p (h t) -> p h t", t=T)
                            chain.count(V.tensor_scalar(den.bitcast(I32), wk[:, :, QB:QB + T].bitcast(I32), 0x7fffffff, None,
                                                        ALU.bitwise_and))
                        dve.wait_ge(dve_chain, chain.n)
                        for j in range(T * h, T * h + 4):
                            chain.count(V.bn_aggr(ml_small[:, 96 + 2 * j:98 + 2 * j], ml_small[:, 48 + 6 * j:54 + 6 * j]))
                        if h:
                            chain.count(V.tensor_tensor(den, den, ml_cols[:, 1].rearrange("p t h -> p h t"), ALU.max))
                        dve.wait_ge(dve_chain, chain.n)
                        if h:
                            chain.link(V.reciprocal(ml_inv, ml_inv))
                            var = ml_var.rearrange("p (h t) -> p h t", t=T)
                            chain.link(V.tensor_tensor(var, ml_moments[:, :, :, 1], den, ALU.mult))
                            V.tensor_tensor(ml_var, ml_var, ml_inv, ALU.mult).then_inc(ml["var_ready"], 1)
                    for t in range(T):
                        chain.count(V.scalar_tensor_tensor(xn[:, t, c], acc[:, t, c], ml_moments[:, h, t, 0:1],
                                                           ml_gate[:, t, c], ALU.subtract, ALU.mult))
                dve.wait_ge(ml["dev_ready"], 1)
                chain.link(V.reciprocal(ml_rs, ml_half))
                chain.link(V.tensor_tensor(ml_scale, ml_rs, ml_inv, ALU.mult))
                for t in range(T):
                    for h in range(M_HEADS):
                        c, j = slice(h * M_DV, (h + 1) * M_DV), T * h + t
                        ins = V.tensor_scalar(xn[:, t, c], xn[:, t, c], ml_scale[:, j:j + 1], None, ALU.mult)
                        ins.then_inc(mixed, 1) if h == M_HEADS - 1 else chain.count(ins)

            def swa_stage(U, outs, nv):
                split_to(U + 4)
                dve.wait_ge(unit_done, U + 2)
                dve.wait_ge(vec_loaded[nv % 3], 16 * (nv // 3 + 1))
                for t in range(T):
                    ins = V.tensor_tensor(swa_kv[:, t, :], wk[:, t, :], vec[:, nv % 3, 0:BANK], ALU.add)
                ins.then_inc(swa_s["rows_kept_v"], 1)
                split_to(U + 6)
                dve.wait_ge(unit_done, U + 6)
                nv += 1
                dve.wait_ge(vec_loaded[nv % 3], 16 * (nv // 3 + 1))
                V.tensor_tensor(work[:, 0:D], acc[:, 0, :], vec[:, nv % 3, :], ALU.add).then_inc(swa_s["rows_kept_v"], 1)
                chain.link(V.tensor_tensor(work[:, D:2 * D], acc[:, 1, :], vec[:, nv % 3, :], ALU.add))
                dve.wait_ge(trig_ready, 1)
                dve.wait_ge(swa_s["roped"], 1)
                rope(V, chain, swa_q[:, :, :, 0:ROPE2], sin2, cos2, ROPE2 // 2, [1]).then_inc(swa_s["roped_v"], 1)
                split_to(U + 7)
                keep_fills(swa_s, range(0, 2), 0, swa_kT, HD, 2)
                keep_fills(swa_s, range(2, 10), 0, swa_qT, HD, 2)
                dve.wait_ge(bias_ready, 3)
                dve.wait_ge(sinks_loaded, 16)
                chain.link(V.tensor_scalar(minus_sinks[:, :], sinks[:, :], -1.0, None, ALU.mult))
                attention(swa_s, HD ** -0.5, window, True, outs)

            def layer_norm(s, end, norms, nv, bias):
                for n in (nv, nv + 1) + ((bias,) if bias is not None else ()):
                    dve.wait_ge(vec_loaded[n % 3], 16 * (n // 3 + 1))
                if bias is not None:
                    for t in range(T):
                        chain.link(V.scalar_tensor_tensor(x[:, t, :], x[:, t, :], ALPHA, vec[:, bias % 3, :], ALU.mult, ALU.add))
                for t in range(T):
                    row = x[:, t, :]
                    wait_result(s, end, t)
                    chain.link(V.scalar_tensor_tensor(row, row, ALPHA if bias is None else 1.0, acc[:, t, :], ALU.mult, ALU.add))
                    halves = stat[:, 40 + 12 * t:52 + 12 * t]
                    chain.count(V.bn_stats(halves[:, 0:6], row[:, 0:BANK]))
                    chain.link(V.bn_stats(halves[:, 6:12], row[:, BANK:D]))
                    mean_var = stat[:, 10 + 2 * t:12 + 2 * t]
                    V.bn_aggr(mean_var, halves).then_inc(var_ready, 1)
                    dve.wait_ge(var_ready, T * norms + t + 1)
                    chain.link(V.scalar_tensor_tensor(row, row, mean_var[:, 0:1], vec[:, nv % 3, :], ALU.subtract, ALU.mult))
                    dve.wait_ge(dev_ready, T * norms + t + 1)
                    y = stat[:, 8 + t:9 + t]
                    chain.link(V.reciprocal(y, stat[:, 2 + t:3 + t]))
                    V.scalar_tensor_tensor(row, row, y, vec[:, (nv + 1) % 3, :], ALU.mult, ALU.add).then_inc(x_ready, 1)

            def ple_stage(U, n, m):
                dve.wait_ge(ple_s["high"], n + 1)
                V.tensor_tensor(hTl[:, 0].rearrange("p k s -> p (k s)"), wk[:, 0, :],
                                hTh[:, 0].rearrange("p k s -> p (k s)").bitcast(F32), ALU.subtract).then_inc(ple_s["kept"], 1)
                keep_turned(m, None)
                split_to(U + 6)

            def ple_out(s, U, n, nv):
                dve.wait_ge(vec_loaded[nv % 3], 16 * (nv // 3 + 1))
                for t in range(T):
                    wait_result(s, U + 4, t)
                    V.tensor_tensor(xn[:, t, :], acc[:, t, :], vec[:, nv % 3, :], ALU.add).then_inc(ple_s["biased"], 1)
                for t in range(T):
                    dve.wait_ge(ple_s["gate"], T * n + t + 1)
                    if t == 0:
                        dve.wait_ge(ple_s["projected"], n + 1)
                    else:
                        dve.wait_ge(unit_done, U + 5)
                    chain.link(V.tensor_tensor(xn[:, t, :], xn[:, t, :],
                                               wk[:, 2 * t:2 * t + 2, :].rearrange("p c n -> p (c n)"), ALU.mult))
                for t in range(T):
                    V.tensor_tensor(x[:, t, :], x[:, t, :], xn[:, t, :], ALU.add).then_inc(x_ready, 1)

            def positions():
                dve.wait_ge(pos_loaded, 32)
                V.tensor_copy(pos_rows[:, :], pos_i[:, :]).then_inc(pos_made, 1)
                dve.wait_ge(pos_turned, 1)
                V.tensor_copy(pos[:, :], wk[:, 2, 0:4]).then_inc(gains_kept, 1)

            def angles():
                dve.wait_ge(gains_kept, 2)
                dve.wait_ge(freq_ready, 24)
                for col, t, f, n in ((0, 0, 0, 16), (16, 1, 0, 16), (32, 2, 16, 8), (40, 3, 16, 8)):
                    chain.link(V.tensor_scalar(angle[:, col:col + n], inv_freq[:, f:f + n], pos[:, t:t + 1], None, ALU.mult))
                chain.link(V.tensor_copy(angle[:, 48:96], angle[:, 0:48]))
                chain.link(V.tensor_scalar(turns[:, 0:48], angle[:, 0:48], INV_TURN, None, ALU.mult))
                chain.link(V.tensor_scalar(turns[:, 48:96], angle[:, 48:96], INV_TURN, 0.25, ALU.mult, ALU.add))
                chain.link(V.tensor_copy(turns_i[:, :], turns[:, :]))
                chain.link(V.tensor_copy(turns[:, :], turns_i[:, :]))
                for part in TURN_PARTS:
                    chain.link(V.scalar_tensor_tensor(angle[:, :], turns[:, :], -part, angle[:, :], ALU.mult, ALU.add))
                chain.link(V.tensor_scalar(angle[:, 48:96], angle[:, 48:96], float(np.pi / 2), None, ALU.add))
                V.tensor_scalar(angle[:, :], angle[:, :], SIN_MAX, -SIN_MAX, ALU.min, ALU.max).then_inc(angles_ready, 1)

            dve.wait_ge(gains_turned, 1)
            V.tensor_copy(gain_cols[:, :], wk[:, 3, 0:NG]).then_inc(gains_kept, 1)
            positions()
            outs = 0
            m = hidden = scaled = norms = nv = 0
            for s, (name, U, n) in enumerate(plan):
                if name in ("ffn", "sb", "mla"):
                    col = {"ffn": (6 * (n // 2) + 4 * (n % 2)), "sb": 2, "mla": 8}[name] * KD
                    rms_in(scaled, m, U, gain_cols[:, col:col + KD])
                    m, scaled = m + 1, scaled + T
                if s == 0:
                    angles()
                if name == "ffn":
                    ffn(U, hidden)
                    hidden += FG
                if name == "sb":
                    sb_stage(U)
                if name == "mla":
                    mla_stage(U, outs)
                if name in ("mlstm", "mlp", "swa"):
                    keep_turned(m, None)
                    split_to(U + RING)
                    m += 1
                if name == "mlp":
                    mlp(U, hidden)
                    hidden += MG
                if name == "mlstm":
                    mlstm_stage(U)
                if name == "swa":
                    swa_stage(U, outs, nv)
                if name == "ple":
                    ple_stage(U, n, m)
                    m += 1
                if name in ("mla", "mlstm", "swa"):
                    keep_turned(m, None)
                    m, outs = m + 1, outs + 1
                    split_to(U + STAGE_UNITS[name] + 1)
                if name in ("ffn", "sb", "mla"):
                    rms_out(scaled, nv)
                    scaled += T
                if name in ("mlstm", "mlp", "swa"):
                    layer_norm(s, U + STAGE_UNITS[name], norms, nv + VECTORS_USED[name] - 2, nv + 2 if name == "swa" else None)
                    norms += 1
                if name == "ple":
                    ple_out(s, U, n, nv)
                nv += VECTORS_USED[name]


def kernel(**inputs):
    import numpy as _np
    import concourse.bacc as _bacc
    from concourse.bass_utils import run_bass_kernel_spmd as _run

    nc = _bacc.Bacc("TRN2", target_bir_lowering=False, num_devices=1)
    arrays, aps = {}, {}
    for name, value in inputs.items():
        v = _np.ascontiguousarray(value)
        arrays[name + "_dram"] = v
        aps[name] = nc.dram_tensor(name + "_dram", v.shape, mybir.dt.from_np(v.dtype), kind="ExternalInput").ap()
    out = nc.dram_tensor("out_dram", (1, S, D), F32, kind="ExternalOutput").ap()
    build(nc, aps, out)
    return _run(nc, [arrays], core_ids=[0]).results[0]["out_dram"]
```
